# Optimizing a Trainium2 kernel written in Bass

```python
import jax, jax.numpy as jnp
from jax import lax
import numpy as np
import math

D_MODEL = 2048
BATCH = 1
SEQ = 256
DEPTH = 2

CHUNK = 64
QBLOCK = 128
N_A_LAYERS = DEPTH // 2
N_B_LAYERS = DEPTH - N_A_LAYERS
EXPAND = 2
W_A = EXPAND * D_MODEL
POOL_WINDOWS = (2, 4, 8, 16)
N_POOL_GROUPS = len(POOL_WINDOWS)
G_A = W_A // N_POOL_GROUPS
N_HEADS = 16
QK_NOPE = 128
QK_ROPE = 64
QK_HEAD = QK_NOPE + QK_ROPE
V_HEAD = 128
KV_LORA = 512
Q_LORA = 512
W_B = N_HEADS * V_HEAD
ROPE_THETA = 10000.0
EPS = 1e-6


def rmsnorm(x, g):
    x32 = x.astype(jnp.float32)
    r = x32 * lax.rsqrt(jnp.mean(x32 * x32, axis=-1, keepdims=True) + EPS)
    return (r * g.astype(jnp.float32)).astype(x.dtype)

def rope_tables(positions):
    inv = ROPE_THETA ** (-jnp.arange(0, QK_ROPE, 2, dtype=jnp.float32) / QK_ROPE)
    ang = positions.astype(jnp.float32)[..., None] * inv
    return jnp.cos(ang), jnp.sin(ang)

def apply_rope(t, cos, sin):
    c = cos[:, :, None, :].astype(t.dtype)
    s = sin[:, :, None, :].astype(t.dtype)
    t1, t2 = t[..., : QK_ROPE // 2], t[..., QK_ROPE // 2:]
    return jnp.concatenate([t1 * c - t2 * s, t2 * c + t1 * s], axis=-1)

def qk_norm_rope(t, g, cos, sin):
    t = rmsnorm(t, g)
    return jnp.concatenate([t[..., :QK_NOPE], apply_rope(t[..., QK_NOPE:], cos, sin)], axis=-1)

def causal_mean_pool(u, w):
    B, S, C = u.shape
    u32 = u.astype(jnp.float32)
    c0 = jnp.concatenate([jnp.zeros((B, 1, C), jnp.float32), jnp.cumsum(u32, axis=1)], axis=1)
    padded = jnp.pad(c0, ((0, 0), (w - 1, 0), (0, 0)))
    window_sum = c0[:, 1:] - padded[:, :S]
    count = jnp.minimum(jnp.arange(1, S + 1, dtype=jnp.float32), float(w))
    return (window_sum / count[None, :, None]).astype(u.dtype)

def pool_mixer_layer(x, norm_g, w_in, w_group, scale, w_out):
    B, S, _ = x.shape
    h = rmsnorm(x, norm_g)
    proj = h @ w_in
    u, gate = proj[..., :W_A], proj[..., W_A:]
    u = u.reshape(B, S, N_POOL_GROUPS, G_A)
    pooled = jnp.stack(
        [causal_mean_pool(u[:, :, gi], w) - u[:, :, gi] for gi, w in enumerate(POOL_WINDOWS)],
        axis=2)
    y = jnp.einsum('bsgc,gcd->bsgd', pooled, w_group).reshape(B, S, W_A) * scale
    y = y * jax.nn.silu(gate)
    return x + y @ w_out

def shared_kv(x, kv_norm_g, kv_w_a, kv_latent_g, kv_w_b, k_norm_g, cos, sin):
    B, S, _ = x.shape
    h = rmsnorm(x, kv_norm_g)
    ckv = h @ kv_w_a
    c, k_rope = ckv[..., :KV_LORA], ckv[..., KV_LORA:]
    c = rmsnorm(c, kv_latent_g)
    kv = (c @ kv_w_b).reshape(B, S, N_HEADS, QK_NOPE + V_HEAD)
    k_nope, v = kv[..., :QK_NOPE], kv[..., QK_NOPE:]
    k_rope = jnp.broadcast_to(k_rope[:, :, None, :], (B, S, N_HEADS, QK_ROPE))
    k = qk_norm_rope(jnp.concatenate([k_nope, k_rope], axis=-1), k_norm_g, cos, sin)
    return k, v

def chunk_causal_attention(q, k, v):
    S = q.shape[1]
    scale = QK_HEAD ** -0.5
    outs = []
    for i in range(S // QBLOCK):
        q0, k_end = i * QBLOCK, (i + 1) * QBLOCK
        s = jnp.einsum('bqhd,bkhd->bhqk', q[:, q0:k_end], k[:, :k_end],
                       preferred_element_type=jnp.float32) * scale
        q_chunk = (q0 + jnp.arange(QBLOCK)) // CHUNK
        k_chunk = jnp.arange(k_end) // CHUNK
        mask = k_chunk[None, :] <= q_chunk[:, None]
        s = jnp.where(mask[None, None], s, -1e30)
        p = jax.nn.softmax(s, axis=-1).astype(v.dtype)
        outs.append(jnp.einsum('bhqk,bkhd->bqhd', p, v[:, :k_end]))
    return jnp.concatenate(outs, axis=1)

def mla_layer(x, k, v, norm_g, w_in, q_latent_g, w_q_b, q_norm_g, w_out, cos, sin):
    B, S, _ = x.shape
    h = rmsnorm(x, norm_g)
    proj = h @ w_in
    q_lat, gate = proj[..., :Q_LORA], proj[..., Q_LORA:]
    q = (rmsnorm(q_lat, q_latent_g) @ w_q_b).reshape(B, S, N_HEADS, QK_HEAD)
    q = qk_norm_rope(q, q_norm_g, cos, sin)
    o = chunk_causal_attention(q, k, v).reshape(B, S, W_B)
    return x + (o * jax.nn.silu(gate)) @ w_out

def first_inputs(seed: int = 0) -> dict:
    key = jax.random.key(seed)
    ks = jax.random.split(key, 24)
    f32 = jnp.float32

    def w(k, shape, fan_in):
        return jax.random.normal(k, shape, f32) * (fan_in ** -0.5)

    def gain(k, shape):
        return 1.0 + 0.02 * jax.random.normal(k, shape, f32)

    x = jax.random.normal(ks[0], (BATCH, SEQ, D_MODEL), f32)
    offsets = jax.random.randint(ks[1], (BATCH,), 0, 64, dtype=jnp.int32) * CHUNK
    positions = (offsets[:, None] + jnp.arange(SEQ, dtype=jnp.int32)[None, :]).astype(jnp.int32)
    return {
        "x": x,
        "positions": positions,
        "a_norm_g": gain(ks[2], (N_A_LAYERS, D_MODEL)),
        "a_w_in": w(ks[3], (N_A_LAYERS, D_MODEL, 2 * W_A), D_MODEL),
        "a_w_group": w(ks[4], (N_A_LAYERS, N_POOL_GROUPS, G_A, G_A), G_A),
        "a_scale": gain(ks[5], (N_A_LAYERS, W_A)),
        "a_w_out": w(ks[6], (N_A_LAYERS, W_A, D_MODEL), W_A),
        "kv_norm_g": gain(ks[7], (D_MODEL,)),
        "kv_w_a": w(ks[8], (D_MODEL, KV_LORA + QK_ROPE), D_MODEL),
        "kv_latent_g": gain(ks[9], (KV_LORA,)),
        "kv_w_b": w(ks[10], (KV_LORA, N_HEADS * (QK_NOPE + V_HEAD)), KV_LORA),
        "k_norm_g": gain(ks[11], (QK_HEAD,)),
        "b_norm_g": gain(ks[12], (N_B_LAYERS, D_MODEL)),
        "b_w_in": w(ks[13], (N_B_LAYERS, D_MODEL, Q_LORA + W_B), D_MODEL),
        "b_q_latent_g": gain(ks[14], (N_B_LAYERS, Q_LORA)),
        "b_w_q_b": w(ks[15], (N_B_LAYERS, Q_LORA, N_HEADS * QK_HEAD), Q_LORA),
        "b_q_norm_g": gain(ks[16], (N_B_LAYERS, QK_HEAD)),
        "b_w_out": w(ks[17], (N_B_LAYERS, W_B, D_MODEL), W_B),
    }

def first_block(x, positions, a_norm_g, a_w_in, a_w_group, a_scale, a_w_out,
              kv_norm_g, kv_w_a, kv_latent_g, kv_w_b, k_norm_g,
              b_norm_g, b_w_in, b_q_latent_g, b_w_q_b, b_q_norm_g, b_w_out):
    cos, sin = rope_tables(positions)
    k = v = None
    for layer in range(DEPTH):
        if layer < N_A_LAYERS:
            x = pool_mixer_layer(x, a_norm_g[layer], a_w_in[layer], a_w_group[layer],
                                 a_scale[layer], a_w_out[layer])
        else:
            if layer == N_A_LAYERS:
                k, v = shared_kv(x, kv_norm_g, kv_w_a, kv_latent_g, kv_w_b, k_norm_g, cos, sin)
            j = layer - N_A_LAYERS
            x = mla_layer(x, k, v, b_norm_g[j], b_w_in[j], b_q_latent_g[j], b_w_q_b[j],
                          b_q_norm_g[j], b_w_out[j], cos, sin)
    return x


DEPTH_2 = 1

HEAD_DIM = 64
A_HEADS = 16
A_KV_HEADS = 2
WINDOW = 128
BLOCK = 128
B_HEADS = 16
KV_RANK = 256
IDX_HEADS = 16
IDX_DIM = 64
TOPK_MAX = 256
NUM_BUCKETS = 32
MAX_DISTANCE = 128
D_FF = 5632
CONV_WIDTH = 3
NEG_INF = -1e30
IDX_SCALE = IDX_DIM ** -0.5 * IDX_HEADS ** -0.5
MIX_WIDTH = (A_HEADS + B_HEADS) * HEAD_DIM

A_Q = A_HEADS * HEAD_DIM
A_KV = A_KV_HEADS * HEAD_DIM
B_Q = B_HEADS * HEAD_DIM
I_Q = IDX_HEADS * IDX_DIM
IN_WIDTH = A_Q + 2 * A_KV + B_Q + KV_RANK + I_Q + IDX_DIM + IDX_HEADS
SPLIT_POINTS = (
    A_Q,
    A_Q + A_KV,
    A_Q + 2 * A_KV,
    A_Q + 2 * A_KV + B_Q,
    A_Q + 2 * A_KV + B_Q + KV_RANK,
    A_Q + 2 * A_KV + B_Q + KV_RANK + I_Q,
    A_Q + 2 * A_KV + B_Q + KV_RANK + I_Q + IDX_DIM,
)


def rms_norm(x, g):
    xf = x.astype(jnp.float32)
    y = xf * lax.rsqrt(jnp.mean(xf * xf, axis=-1, keepdims=True) + EPS)
    return (y * g.astype(jnp.float32)).astype(x.dtype)

def rel_bucket(dist):
    n = jnp.maximum(dist, 0)
    max_exact = NUM_BUCKETS // 2
    nf = jnp.maximum(n, 1).astype(jnp.float32)
    large = max_exact + (jnp.log(nf / max_exact) / math.log(MAX_DISTANCE / max_exact)
                         * (NUM_BUCKETS - max_exact)).astype(jnp.int32)
    large = jnp.minimum(large, NUM_BUCKETS - 1)
    return jnp.where(n < max_exact, n, large)

def swa_attention(q, k, v, sinks, rel_table):
    Bsz, T, H, D = q.shape
    nblk = T // BLOCK
    G = H // A_KV_HEADS
    qb = q.reshape(Bsz, nblk, BLOCK, A_KV_HEADS, G, D)
    pad = ((0, 0), (BLOCK, 0), (0, 0), (0, 0))
    kp = jnp.pad(k, pad).reshape(Bsz, nblk + 1, BLOCK, A_KV_HEADS, D)
    vp = jnp.pad(v, pad).reshape(Bsz, nblk + 1, BLOCK, A_KV_HEADS, D)
    kb = jnp.concatenate([kp[:, :-1], kp[:, 1:]], axis=2)
    vb = jnp.concatenate([vp[:, :-1], vp[:, 1:]], axis=2)
    s = jnp.einsum('bnqkgd,bnskd->bnkgqs', qb, kb).astype(jnp.float32) * (D ** -0.5)
    i = jnp.arange(BLOCK, dtype=jnp.int32)[:, None]
    j = jnp.arange(2 * BLOCK, dtype=jnp.int32)[None, :]
    dist = i + BLOCK - j
    in_window = (dist >= 0) & (dist < WINDOW)
    key_pos = jnp.arange(nblk, dtype=jnp.int32)[:, None, None] * BLOCK - BLOCK + j[None]
    valid = in_window[None] & (key_pos >= 0)
    bias = jnp.transpose(rel_table[rel_bucket(dist)], (2, 0, 1))
    bias = bias.reshape(A_KV_HEADS, G, BLOCK, 2 * BLOCK).astype(jnp.float32)
    s = jnp.where(valid[None, :, None, None], s + bias[None, None], NEG_INF)
    sink = sinks.astype(jnp.float32).reshape(A_KV_HEADS, G)[None, None, :, :, None, None]
    m = jnp.maximum(jnp.max(s, axis=-1, keepdims=True), sink)
    e = jnp.exp(s - m)
    p = e / (jnp.sum(e, axis=-1, keepdims=True) + jnp.exp(sink - m))
    o = jnp.einsum('bnkgqs,bnskd->bnqkgd', p.astype(v.dtype), vb)
    return o.reshape(Bsz, T, H * D)

def dsa_attention(q, c_kv, w_uk, w_uv, q_idx, k_idx, w_idx, rel_table):
    Bsz, T, H, D = q.shape
    nblk = T // BLOCK
    topk = min(TOPK_MAX, T // 4)
    scale = D ** -0.5
    key_pos = jnp.arange(T, dtype=jnp.int32)

    def one_block(blk):
        start = blk * BLOCK
        qpos = start + jnp.arange(BLOCK, dtype=jnp.int32)
        qi = lax.dynamic_slice_in_dim(q_idx, start, BLOCK, axis=1)
        wi = lax.dynamic_slice_in_dim(w_idx, start, BLOCK, axis=1)
        qb = lax.dynamic_slice_in_dim(q, start, BLOCK, axis=1)
        dots = jnp.einsum('bqhd,bsd->bqhs', qi, k_idx).astype(jnp.float32)
        index_score = jnp.einsum('bqh,bqhs->bqs', wi.astype(jnp.float32),
                                 jax.nn.relu(dots)) * IDX_SCALE
        causal = key_pos[None, :] <= qpos[:, None]
        index_score = jnp.where(causal[None], index_score, NEG_INF)
        _, sel = lax.top_k(index_score, topk)
        c_sel = jax.vmap(lambda ck, ix: ck[ix])(c_kv, sel)
        q_lat = jnp.einsum('bqhd,hrd->bqhr', qb, w_uk)
        s = jnp.einsum('bqhr,bqkr->bqhk', q_lat, c_sel).astype(jnp.float32) * scale
        dist = qpos[None, :, None] - sel
        bias = jnp.moveaxis(rel_table[rel_bucket(dist)], -1, 2).astype(jnp.float32)
        s = jnp.where((dist >= 0)[:, :, None, :], s + bias, NEG_INF)
        p = jax.nn.softmax(s, axis=-1).astype(c_sel.dtype)
        o_lat = jnp.einsum('bqhk,bqkr->bqhr', p, c_sel)
        o = jnp.einsum('bqhr,hrd->bqhd', o_lat, w_uv)
        return o.reshape(Bsz, BLOCK, H * D)

    out = lax.map(one_block, jnp.arange(nblk, dtype=jnp.int32))
    return jnp.transpose(out, (1, 0, 2, 3)).reshape(Bsz, T, H * D)

def conv_ffn(h, w_up, conv_w, conv_b, w_down):
    u, g = jnp.split(h @ w_up, 2, axis=-1)
    u = lax.conv_general_dilated(
        u, conv_w[:, None, :], window_strides=(1,), padding=((CONV_WIDTH - 1, 0),),
        dimension_numbers=('NWC', 'WIO', 'NWC'), feature_group_count=D_FF) + conv_b
    return (jax.nn.silu(u) * g) @ w_down

def second_inputs(seed: int = 0) -> dict:
    key = jax.random.key(seed)
    ks = jax.random.split(key, 20)
    f32 = jnp.float32
    nrm = lambda k, shape, s: jax.random.normal(k, shape, f32) * s
    return {
        "x": nrm(ks[0], (BATCH, SEQ, D_MODEL), 1.0),
        "c": nrm(ks[1], (BATCH, D_MODEL), 1.0),
        "w_mod": nrm(ks[2], (DEPTH_2, D_MODEL, 6 * D_MODEL), D_MODEL ** -0.5),
        "b_mod": nrm(ks[3], (DEPTH_2, 6 * D_MODEL), 0.02),
        "norm_attn": 1.0 + nrm(ks[4], (DEPTH_2, D_MODEL), 0.02),
        "w_in": nrm(ks[5], (DEPTH_2, D_MODEL, IN_WIDTH), D_MODEL ** -0.5),
        "attn_sinks": nrm(ks[6], (DEPTH_2, A_HEADS), 0.5),
        "kv_norm": 1.0 + nrm(ks[7], (DEPTH_2, KV_RANK), 0.02),
        "w_uk": nrm(ks[8], (DEPTH_2, B_HEADS, KV_RANK, HEAD_DIM), KV_RANK ** -0.5),
        "w_uv": nrm(ks[9], (DEPTH_2, B_HEADS, KV_RANK, HEAD_DIM), KV_RANK ** -0.5),
        "rel_bias": nrm(ks[10], (NUM_BUCKETS, A_HEADS + B_HEADS), 0.3),
        "w_out": nrm(ks[11], (DEPTH_2, MIX_WIDTH, D_MODEL), MIX_WIDTH ** -0.5),
        "norm_ffn": 1.0 + nrm(ks[12], (DEPTH_2, D_MODEL), 0.02),
        "w_up": nrm(ks[13], (DEPTH_2, D_MODEL, 2 * D_FF), D_MODEL ** -0.5),
        "conv_w": nrm(ks[14], (DEPTH_2, CONV_WIDTH, D_FF), CONV_WIDTH ** -0.5),
        "conv_b": nrm(ks[15], (DEPTH_2, D_FF), 0.02),
        "w_down": nrm(ks[16], (DEPTH_2, D_FF, D_MODEL), D_FF ** -0.5),
        "norm_final": 1.0 + nrm(ks[17], (D_MODEL,), 0.02),
    }

def second_block(x, c, w_mod, b_mod, norm_attn, w_in, attn_sinks, kv_norm, w_uk, w_uv,
              rel_bias, w_out, norm_ffn, w_up, conv_w, conv_b, w_down, norm_final):
    Bsz, T, _ = x.shape
    rel_a = rel_bias[:, :A_HEADS]
    rel_b = rel_bias[:, A_HEADS:]
    c_act = jax.nn.silu(c)
    for l in range(DEPTH_2):
        mod = c_act @ w_mod[l] + b_mod[l]
        sh1, sc1, g1, sh2, sc2, g2 = [m[:, None, :] for m in jnp.split(mod, 6, axis=-1)]

        h = rms_norm(x, norm_attn[l]) * (1.0 + sc1) + sh1
        qa, ka, va, qb, ckv, qi, ki, wi = jnp.split(h @ w_in[l], SPLIT_POINTS, axis=-1)
        qa = qa.reshape(Bsz, T, A_HEADS, HEAD_DIM)
        ka = ka.reshape(Bsz, T, A_KV_HEADS, HEAD_DIM)
        va = va.reshape(Bsz, T, A_KV_HEADS, HEAD_DIM)
        qb = qb.reshape(Bsz, T, B_HEADS, HEAD_DIM)
        ckv = rms_norm(ckv, kv_norm[l])
        qi = qi.reshape(Bsz, T, IDX_HEADS, IDX_DIM)
        out_a = swa_attention(qa, ka, va, attn_sinks[l], rel_a)
        out_b = dsa_attention(qb, ckv, w_uk[l], w_uv[l], qi, ki, wi, rel_b)
        mix = jnp.concatenate([out_a, out_b], axis=-1) @ w_out[l]
        x = x + g1 * mix

        h = rms_norm(x, norm_ffn[l]) * (1.0 + sc2) + sh2
        x = x + g2 * conv_ffn(h, w_up[l], conv_w[l], conv_b[l], w_down[l])
    return rms_norm(x, norm_final)


def setup_inputs(seed=0):
    out = dict(first_inputs(seed))
    for name, value in second_inputs(seed + 1).items():
        if name != "x":
            out[name + "_2"] = value
    return out


def reference(
    x, positions, a_norm_g, a_w_in, a_w_group, a_scale, a_w_out, kv_norm_g, kv_w_a, kv_latent_g,
    kv_w_b, k_norm_g, b_norm_g, b_w_in, b_q_latent_g, b_w_q_b, b_q_norm_g, b_w_out, c_2,
    w_mod_2, b_mod_2, norm_attn_2, w_in_2, attn_sinks_2, kv_norm_2, w_uk_2, w_uv_2, rel_bias_2,
    w_out_2, norm_ffn_2, w_up_2, conv_w_2, conv_b_2, w_down_2, norm_final_2,
):
    x = first_block(
        x, positions, a_norm_g, a_w_in, a_w_group, a_scale, a_w_out, kv_norm_g, kv_w_a,
        kv_latent_g, kv_w_b, k_norm_g, b_norm_g, b_w_in, b_q_latent_g, b_w_q_b, b_q_norm_g,
        b_w_out,
    )
    return second_block(
        x, c_2, w_mod_2, b_mod_2, norm_attn_2, w_in_2, attn_sinks_2, kv_norm_2, w_uk_2, w_uv_2,
        rel_bias_2, w_out_2, norm_ffn_2, w_up_2, conv_w_2, conv_b_2, w_down_2, norm_final_2,
    )


_drawn_inputs = setup_inputs


def setup_inputs(seed=0):
    import zlib

    import numpy as np

    out = dict(_drawn_inputs(seed))
    spreads = {}
    factors = {'a_norm_g': 3.294,
     'a_scale': 4.562,
     'kv_norm_g': 8.0,
     'kv_latent_g': 8.0,
     'k_norm_g': 8.0,
     'b_norm_g': 8.0,
     'b_q_latent_g': 8.0,
     'b_q_norm_g': 8.0,
     'norm_attn_2': 17.196,
     'attn_sinks_2': 64.0,
     'kv_norm_2': 64.0,
     'norm_ffn_2': 33.792,
     'conv_b_2': 62.104,
     'norm_final_2': 7.812,
     'b_mod_2': 3.54,
     'rel_bias_2': 8.0}
    for name, (base, spread) in spreads.items():
        noise = np.random.default_rng([zlib.crc32(name.encode()), seed]).standard_normal(out[name].shape)
        drawn = base * np.exp(spread * noise) if base else spread * noise
        out[name] = __import__('jax').numpy.asarray(drawn.astype(out[name].dtype))
    for name, factor in factors.items():
        out[name] = (out[name] * factor).astype(out[name].dtype)
    return out
```

```python
from contextlib import ExitStack, contextmanager

import numpy as np

import concourse.bass as bass
from concourse import mybir

F32 = mybir.dt.float32
F32R = mybir.dt.float32r
I32 = mybir.dt.int32
ALU = mybir.AluOpType
ACT = mybir.ActivationFunctionType
AX = mybir.AxisListType

P = 128
TOK = 256
HALVES = TOK // P
D = 2048
KD = D // P
EPS = 1e-6
NEG = -1e30

POOL_WINDOWS = (2, 4, 8, 16)
GROUPS = len(POOL_WINDOWS)
W_A = 2 * D
G_A = W_A // GROUPS
PAD = max(POOL_WINDOWS)
HEADS = 16
NOPE, ROPE, VD, LORA = 128, 64, 128, 512
QK = NOPE + ROPE
CHUNK = 64
PAIRS = HEADS // 2

HD = 64
TILES = HEADS * HD // P
RANK = 256
TOPK = 64
WINDOW = 128
BUCKETS = 32
DFF = 5632
KF = DFF // P
FBLOCKS = DFF // 512
IDX_SCALE = HD ** -0.5 * HEADS ** -0.5
COL_QA, COL_KA, COL_VA, COL_QB, COL_C, COL_QI, COL_KW = 0, 1024, 1152, 1280, 2304, 2560, 3584
KW = HD + HEADS
T_KA, T_VA, T_QB, T_C, T_QI = COL_KA // P, COL_VA // P, COL_QB // P, COL_C // P, COL_QI // P
PROJ = COL_KW // P
N_VEC = 29

RING = 4
SLAB_K = 2
SLAB_N = 512
SLAB = SLAB_K * SLAB_N
SC = P + TOK

V_A_NORM, V_A_SCALE, V_KV_NORM, V_KV_LAT, V_B_NORM, V_Q_LAT = 0, 16, 48, 64, 68, 84
V_NORM_ATTN, V_C, V_KV_NORM2, V_KN, V_QN, V_KR, V_QR, V_KRS, V_QRS = 88, 104, 120, 122, 123, 124, 125, 126, 127
V_BMOD, V_NORM_FFN, V_NORM_FIN, V_CONV, V_CONVB = 128, 224, 240, 256, 256 + 3 * KF
V_ROWS = V_CONVB + KF

TWO_PI_A = 6.28125
TWO_PI_B = float(np.float32(np.round((2 * np.pi - TWO_PI_A) * 2 ** 21) / 2 ** 21))
TWO_PI_C = float(2 * np.pi - TWO_PI_A - TWO_PI_B)
ROUND = 1.5 * 2 ** 23
PI_CLAMP = 3.1415925


def constants():
    q = np.arange(P)[:, None]
    parts = {}
    parts["ident"] = np.eye(P)
    parts["dup0"] = (np.arange(P)[:, None] == np.arange(P)[None] % HD)
    parts["dup1"] = (np.arange(P)[:, None] == HD + np.arange(P)[None] % HD)
    k0, k1 = np.arange(P)[None], np.arange(TOK)[None]
    parts["chunk_mask"] = np.concatenate([np.where(k0 // CHUNK <= q // CHUNK, 0, NEG),
                                          np.where(k1 // CHUNK <= (q + P) // CHUNK, 0, NEG)], 1)
    dist = q + P - k1
    parts["window_mask"] = np.where((dist >= 0) & (dist < WINDOW), 0, NEG)
    parts["causal_mask"] = np.where(dist >= 0, 0, NEG)
    t = np.arange(PAD)
    parts["rcount"] = np.tile(np.concatenate([1 / np.minimum(t + 1, w) for w in POOL_WINDOWS])[None], (P, 1))
    parts["rwindow"] = np.tile(np.array([1 / w for w in POOL_WINDOWS])[None], (P, 1))
    parts["inv_freq"] = np.tile(np.float32(10000.0) ** (-np.arange(0, ROPE, 2, dtype=np.float32) / np.float32(ROPE)), 4)[:, None]
    parts["rope_sign"] = np.where(np.arange(P) % ROPE < ROPE // 2, -1.0, 1.0)[:, None]
    n = TOK - 1 - np.arange(SC)
    exact = BUCKETS // 2
    large = exact + (np.log(np.maximum(n, 1).astype(np.float32) / exact) / np.log(128 / exact) * (BUCKETS - exact)).astype(np.int32)
    bucket = np.where(n < exact, n, np.minimum(large, BUCKETS - 1))
    onehot = np.zeros((P, SC))
    onehot[bucket[n >= 0], np.arange(SC)[n >= 0]] = 1
    parts["onehot"] = onehot
    cols, at = {}, 0
    for name, a in parts.items():
        cols[name] = (at, at + a.shape[1])
        at += a.shape[1]
    return np.ascontiguousarray(np.concatenate([a.astype(np.float32) for a in parts.values()], 1)), cols


class Count:

    def __init__(self):
        self.base, self.k, self.i, self.per = 0, 0, None, 0

    def enter(self, i, per):
        self.i, self.per, self.base, self.k = i, per, self.base + self.k, 0

    def leave(self, n):
        assert self.k == self.per, (self.k, self.per)
        self.base, self.k, self.i = self.base + n * self.per, 0, None

    def step(self, n=1):
        self.k += n

    def value(self, add=0):
        v = self.base + self.k + add
        return v if self.i is None else self.i * self.per + v

    def total(self):
        assert self.i is None
        return self.base + self.k

    def slot(self, ring):
        assert self.i is None or self.per % ring == 0
        return (self.base + self.k) % ring

    def turn(self, ring, add=0):
        v = (self.base + self.k) // ring + add
        return v if self.i is None else self.i * (self.per // ring) + v


@contextmanager
def loop(eng, n, counts):
    with eng.Fori(0, n) as i:
        for c, per in counts:
            c.enter(i, per)
        yield i
        for c, _ in counts:
            c.leave(n)


def two_block_kernel(nc, t, out, cols):
    fixed = ExitStack()
    with fixed:
        def sb(name, shape, dt=F32, scope=fixed):
            return scope.enter_context(nc.sbuf_tensor(name, shape, dt))

        def sem(name):
            return fixed.enter_context(nc.semaphore(name))

        xT = sb("xT", [P, KD, TOK])
        h_hi = sb("h_hi", [P, KD, TOK], F32R)
        h_lo = sb("h_lo", [P, KD, TOK], F32R)
        raw = [sb(f"raw{s}", [P, SLAB]) for s in range(RING)]
        w_hi = [sb(f"w_hi{s}", [P, SLAB], F32R) for s in range(RING)]
        w_lo = [sb(f"w_lo{s}", [P, SLAB], F32R) for s in range(RING)]
        tmp = [sb(f"tmp{s}", [P, 4, TOK]) for s in range(2)]
        table = sb("table", [P, t["consts"].shape[1]])
        vec = sb("vec", [P, V_ROWS])
        ones = sb("ones", [P, TOK])
        eps = sb("eps", [P, 1])
        rms_std = sb("rms_std", [P, TOK])
        rms_inv = sb("rms_inv", [P, TOK])
        mod = sb("mod", [P, 6, KD])
        gain1 = sb("gain1", [P, KD])
        gain2 = sb("gain2", [P, KD])
        silu_c = sb("silu_c", [P, KD])
        rel = sb("rel", [BUCKETS, 2 * HEADS])
        lines = sb("lines", [2 * HEADS, SC])
        pos = sb("pos", [ROPE, TOK], I32)
        cos = sb("cos", [ROPE, TOK])
        sin = sb("sin", [ROPE, TOK])

        def tab(name, a=0, b=None, rows=P):
            lo, hi = cols[name]
            return table[0:rows, lo + a:(hi if b is None else lo + b)]

        acc = [fixed.enter_context(nc.psum_tensor(f"acc{s}", [P, 4, TOK], F32)) for s in range(2)]
        sums = fixed.enter_context(nc.psum_tensor("sums", [P, 2, 512], F32))
        side = fixed.enter_context(nc.psum_tensor("side", [P, 2, 512], F32))
        rms_sum, lat_sum = sums[:, 0, 0:TOK], sums[:, 1, 0:TOK]
        acc_banks = [a[:, :, :].rearrange("p (b j) t -> p b (j t)", b=2) for a in acc]
        bias_lines = nc.dram_tensor("bias_lines", [2 * HEADS, P, SC], F32)

        mod_scope = ExitStack()
        mod_raw = [sb(f"mod_raw{s}", [P, 1024], F32, mod_scope) for s in range(2)]
        mod_acc = sb("mod_acc", [P, D], F32, mod_scope)

        with ExitStack() as scope:
            x_tok = sb("x_tok", [P, HALVES, D], F32, scope)
            rows = [sb(f"vec_rows{s}", [P, P], F32, scope) for s in range(4)]
            angle = sb("angle", [ROPE, 4, TOK], F32, scope)
        with ExitStack() as scope:
            pool_hi = sb("pool_hi", [P, 8, TOK], F32R, scope)
            pool_lo = sb("pool_lo", [P, 8, TOK], F32R, scope)
            y_hi = sb("y_hi", [P, 8, TOK], F32R, scope)
            y_lo = sb("y_lo", [P, 8, TOK], F32R, scope)
            gate_a = sb("gate_a", [P, 8, TOK], F32, scope)
            csum = sb("csum", [P, 4, PAD + TOK], F32, scope)
            first16 = sb("first16", [P, 4, PAD], F32, scope)
        with ExitStack() as scope:
            c_hi = sb("c_hi", [P, 4, TOK], F32R, scope)
            c_lo = sb("c_lo", [P, 4, TOK], F32R, scope)
            q_hi = sb("q_hi", [P, 4, TOK], F32R, scope)
            q_lo = sb("q_lo", [P, 4, TOK], F32R, scope)
            gate_b = sb("gate_b", [P, HEADS, TOK], F32, scope)
            kr_swap = sb("kr_swap", [ROPE, TOK], F32, scope)
            kr_rot = sb("kr_rot", [ROPE, TOK], F32, scope)
            kr_sq = sb("kr_sq", [ROPE, TOK], F32, scope)
            kq = [sb(f"kq{s}", [P, 4, TOK], F32, scope) for s in range(2)]
            qr = [sb(f"qr{s}", [ROPE, 2, TOK], F32, scope) for s in range(2)]
            kr = [sb(f"kr{s}", [ROPE, 2, TOK], F32, scope) for s in range(2)]
            vs = [sb(f"vs{s}", [P, HALVES, 2 * VD], F32, scope) for s in range(2)]
            qr_swap = sb("qr_swap", [ROPE, 2, TOK], F32, scope)
            qr_sq = sb("qr_sq", [ROPE, 2, TOK], F32, scope)
            m_prob = sb("m_prob", [P, 2, SC], F32, scope)
            m_probT = sb("m_probT", [P, 2, SC], F32, scope)
            m_out = sb("m_out", [P, 2, TOK], F32, scope)
            m_max = sb("m_max", [P, 2, 2], F32, scope)
            m_neg = sb("m_neg", [P, 2, 2], F32, scope)
            m_sum = sb("m_sum", [P, 2, 2], F32, scope)
            m_inv = sb("m_inv", [P, 2, 2], F32, scope)
        mod_scope.close()
        with ExitStack() as scope:
            proj = sb("proj", [P, PROJ, TOK], F32, scope)
            bias = sb("bias", [P, HEADS, TOK], F32, scope)
            kiwi = sb("kiwi", [KW, TOK], F32, scope)
            ki_dup = sb("ki_dup", [P, TOK], F32, scope)
            ka_dup = sb("ka_dup", [P, 2, TOK], F32, scope)
            va_tok = sb("va_tok", [P, HALVES, 2 * HD], F32, scope)
            wi_tok = sb("wi_tok", [P, HALVES, HEADS], F32, scope)
            lat_hi = sb("lat_hi", [P, 2, TOK], F32R, scope)
            lat_lo = sb("lat_lo", [P, 2, TOK], F32R, scope)
            kb = sb("kb", [P, TILES, TOK], F32, scope)
            vb_tok = sb("vb_tok", [P, HALVES, HEADS * HD], F32, scope)
            q_st = [sb(f"q_st{s}", [P, TOK], F32, scope) for s in range(2)]
            k_st = [sb(f"k_st{s}", [P, TOK], F32, scope) for s in range(2)]
            v_st = [sb(f"v_st{s}", [P, HALVES, 2, HD], F32, scope) for s in range(2)]
            prob = [sb(f"prob{s}", [P, 2, SC], F32, scope) for s in range(2)]
            probT = sb("probT", [P, 2, SC], F32, scope)
            sinks = sb("sinks", [P, HEADS], F32, scope)
            idx, idx_work = probT[:, 0, :], prob[1][:, 0, :]
            sel = sb("sel", [P, SC], F32, scope)
            top8 = sb("top8", [P, HALVES, 8], F32, scope)
            quota = sb("quota", [P, HALVES], F32, scope)
            a_max = [sb(f"a_max{s}", [P, 2, 2], F32, scope) for s in range(2)]
            a_neg = [sb(f"a_neg{s}", [P, 2, 2], F32, scope) for s in range(2)]
            a_sum = [sb(f"a_sum{s}", [P, 2, 2], F32, scope) for s in range(2)]
            a_gap = [sb(f"a_gap{s}", [P, 2, 2], F32, scope) for s in range(2)]
            a_exp = [sb(f"a_exp{s}", [P, 2, 2], F32, scope) for s in range(2)]
            a_inv = sb("a_inv", [P, 2, 2], F32, scope)
        with ExitStack() as scope:
            conv = sb("conv", [P, 4, TOK], F32, scope)
            conv_silu = sb("conv_silu", [P, 4, TOK], F32, scope)
            f_raw = sb("f_raw", [P, 4, TOK], F32, scope)
            f_hi = [sb(f"f_hi{s}", [P, 4, TOK], F32R, scope) for s in range(2)]
            f_lo = [sb(f"f_lo{s}", [P, 4, TOK], F32R, scope) for s in range(2)]
            y_tok = [sb(f"y_tok{s}", [P, HALVES, 512], F32, scope) for s in range(2)]

        raw_landed = [sem(f"raw_landed{s}") for s in range(RING)]
        hi_ready = sem("hi_ready")
        lo_ready = sem("lo_ready")
        slab_used = sem("slab_used")
        acc_taken = [sem(f"acc_taken{s}") for s in range(2)]
        table_in, vec_in, x_in, rel_in, pos_in, bias_in, bias_out, sinks_in = map(sem, (
            "table_in", "vec_in", "x_in", "rel_in", "pos_in", "bias_in", "bias_out", "sinks_in"))
        const_set, x_turned, vec_turned, vec_ready, line_sum, line_ready = map(sem, (
            "const_set", "x_turned", "vec_turned", "vec_ready", "line_sum", "line_ready"))
        x_ready = sem("x_ready")
        sq_ready, sq_summed, std_ready, norm_ready, h_hi_ready, h_lo_ready = map(sem, (
            "sq_ready", "sq_summed", "std_ready", "norm_ready", "h_hi_ready", "h_lo_ready"))
        pool_ready, pool_hi_ready, pool_lo_ready = map(sem, ("pool_ready", "pool_hi_ready", "pool_lo_ready"))
        y_hi_ready, y_lo_ready = map(sem, ("y_hi_ready", "y_lo_ready"))
        csilu_ready, mod_summed, mod_ready = map(sem, ("csilu_ready", "mod_summed", "mod_ready"))
        mod_landed = [sem(f"mod_landed{s}") for s in range(2)]
        lat_sq, lat_stat, lat_std, lat_norm, lat_hi_ready, lat_lo_ready = map(sem, (
            "lat_sq", "lat_stat", "lat_std", "lat_norm", "lat_hi_ready", "lat_lo_ready"))
        angle_ready, trig_ready, kr_ready, kr_done = map(sem, ("angle_ready", "trig_ready", "kr_ready", "kr_done"))
        m_sq, m_stat, m_std, m_qk, m_score, m_max_ready, m_exp, m_prob_ready, m_turned, m_turned_in, m_pv, m_out_ready, \
            m_mix_hi, mix_lo = map(sem, ("m_sq", "m_stat", "m_std", "m_qk", "m_score", "m_max_ready", "m_exp", "m_prob_ready",
                                         "m_turned", "m_turned_in", "m_pv", "m_out_ready", "m_mix_hi", "mix_lo"))
        side_done, side_taken, bias_ready = map(sem, ("side_done", "side_taken", "bias_ready"))
        idx_staged, idx_dots, idx_relu, idx_added, sel_ready = map(sem, (
            "idx_staged", "idx_dots", "idx_relu", "idx_added", "sel_ready"))
        att = []
        for kind in ("win", "sel"):
            att.append({n: sem(f"{kind}_{n}") for n in (
                "staged", "score", "max", "exp", "prob", "turned", "turned_in", "pv", "mix_hi", "mix_lo")})
        conv_silu_ready, f_hi_ready, f_lo_ready = map(sem, ("conv_silu_ready", "f_hi_ready", "f_lo_ready"))
        fin_ready, fin_turned = sem("fin_ready"), sem("fin_turned")
        y_stored = [sem(f"y_stored{s}") for s in range(2)]
        y_copied = sem("y_copied")
        dve_step = sem("dve_step")
        mod_started = sem("mod_started")
        mod_step = sem("mod_step")

        block = fixed.enter_context(nc.Block())

        def f32(ap):
            return ap.bitcast(F32)

        def flat(ap):
            return ap.rearrange("p a b -> p (a b)")

        @block.sync
        def _(sp):
            slabs = Count()

            def load(src, k, n):
                sp.wait_ge(lo_ready, slabs.value(1))
                s = slabs.slot(RING)
                sp.dma_start(raw[s][:, 0:k * n].rearrange("p (k n) -> p k n", k=k),
                             src.rearrange("(k p) n -> p k n", p=P)).then_inc(raw_landed[s], 16)
                slabs.step()

            def stream(w, rows, row0, col0, n=SLAB_N):
                for r in range(0, rows, SLAB_K * P):
                    load(w[bass.ds(row0 + r, SLAB_K * P), bass.ds(col0, n)], SLAB_K, n)

            sp.dma_start(table[:, :], t["consts"][:, :]).then_inc(table_in, 16)
            sp.dma_start(x_tok[:, :, :], t["x"][0].rearrange("(h p) d -> p h d", p=P)).then_inc(x_in, 16)
            a_in, a_out = t["a_w_in"][0], t["a_w_out"][0]
            a_group = t["a_w_group"][0].rearrange("g c d -> (g c) d")
            with loop(sp, GROUPS, [(slabs, 56)]) as g:
                for half in range(2):
                    stream(a_in, D, 0, g * G_A + half * SLAB_N)
                for half in range(2):
                    stream(a_in, D, 0, g * G_A + (W_A + half * SLAB_N))
                for half in range(2):
                    stream(a_group, G_A, g * G_A, half * SLAB_N)
                for m in range(4):
                    stream(a_out, G_A, g * G_A, m * SLAB_N)
            stream(t["kv_w_a"], D, 0, 0)
            load(t["kv_w_a"][:, LORA:LORA + ROPE], KD, ROPE)
            stream(t["b_w_in"][0], D, 0, 0)
            with loop(sp, 2, [(slabs, 16)]) as i:
                for m in range(2):
                    stream(t["b_w_in"][0], D, 0, i * 1024 + (m + 1) * SLAB_N)

            def pair(p):
                stream(t["kv_w_b"], LORA, 0, p * 512)
                stream(t["b_w_q_b"][0], LORA, 0, p * 384, 384)

            with loop(sp, PAIRS // 2, [(slabs, 8)]) as i:
                pair(i * 2)
                pair(i * 2 + 1)
            for w in (t["b_w_out"][0],):
                with loop(sp, 2, [(slabs, 16)]) as i:
                    for m in range(2):
                        stream(w, D, 0, i * 1024 + m * SLAB_N)
            w_in = t["w_in_2"][0]
            with loop(sp, 3, [(slabs, 16)]) as i:
                for m in range(2):
                    stream(w_in, D, 0, i * 1024 + m * SLAB_N)
            stream(w_in, D, 0, 6 * SLAB_N)
            for r in range(2):
                load(w_in[r * 1024:(r + 1) * 1024, COL_KW:COL_KW + KW], 8, KW)

            for w in (t["w_uk_2"], t["w_uv_2"]):
                for r in range(RANK // P):
                    sp.wait_ge(lo_ready, slabs.value(1))
                    s = slabs.slot(RING)
                    sp.dma_start(raw[s][:, :].rearrange("p (h d) -> p h d", d=HD),
                                 w[0, :, r * P:(r + 1) * P, :].rearrange("h p d -> p h d")).then_inc(raw_landed[s], 16)
                    slabs.step()
            with loop(sp, 2, [(slabs, 16)]) as i:
                for m in range(2):
                    stream(t["w_out_2"][0], D, 0, i * 1024 + m * SLAB_N)
            up, down = t["w_up_2"][0], t["w_down_2"][0]

            def ff_up(i):
                stream(up, D, 0, i * SLAB_N)
                stream(up, D, 0, i * SLAB_N + DFF)

            def ff_down(i):
                for m in range(4):
                    stream(down, SLAB_N, i * SLAB_N, m * SLAB_N)

            ff_up(0)
            with loop(sp, FBLOCKS // 2, [(slabs, 48)]) as i:
                for a in range(2):
                    ff_up(i * 2 + (a + 1))
                    ff_down(i * 2 + a)
            ff_down(FBLOCKS - 1)
            out_v = out[0].rearrange("(h p) d -> p h d", p=P)
            for m in range(4):
                sp.wait_ge(y_copied, m + 1)
                sp.dma_start(out_v[:, :, m * 512:(m + 1) * 512], y_tok[m % 2][:, :, :]).then_inc(y_stored[m % 2], 16)
            for s in range(2):
                sp.wait_ge(y_stored[s], 32)

        @block.gpsimd
        def _(gp):
            gp.wait_ge(csilu_ready, 1)
            w_mod = t["w_mod_2"][0]
            slabs, steps = Count(), Count()

            def mod_load(v, j):
                s = j % 2
                gp.dma_start(mod_raw[s][:, :], w_mod[(j // 2) * P:(j // 2 + 1) * P, bass.ds(v * D + (j % 2) * 1024, 1024)])\
                    .then_inc(mod_landed[s], 16)

            with loop(gp, 6, [(slabs, 2 * KD), (steps, 4 * KD - 2)]) as v:
                mod_load(v, 0)
                mod_load(v, 1)
                gp.wait_ge(mod_ready, v + 1)
                for j in range(2 * KD):
                    s, k = j % 2, j // 2
                    a = mod_acc[:, s * 1024:(s + 1) * 1024]
                    gp.wait_ge(mod_landed[s], slabs.turn(2, 1) * 16)
                    gp.sem_inc(mod_started, 1)
                    slabs.step()
                    if k == 0:
                        gp.tensor_scalar(a, mod_raw[s][:, :], silu_c[:, 0:1], 1.0, ALU.mult, ALU.mult).then_inc(mod_step, 1)
                        steps.step()
                    else:
                        gp.tensor_scalar(mod_raw[s][:, :], mod_raw[s][:, :], silu_c[:, k:k + 1], 1.0, ALU.mult, ALU.mult)\
                            .then_inc(mod_step, 1)
                        steps.step()
                        gp.wait_ge(mod_step, steps.value())
                        gp.tensor_tensor(a, a, mod_raw[s][:, :], ALU.add).then_inc(mod_step, 1)
                        steps.step()
                    gp.wait_ge(mod_step, steps.value())
                    if j + 2 < 2 * KD:
                        mod_load(v, j + 2)

            def bias_mask(kind, n):
                gp.wait_ge(bias_in, 16 * (n + 1))
                gp.tensor_tensor(bias[:, :, :], bias[:, :, :],
                                 tab(kind).unsqueeze(1).broadcast_to([P, HEADS, TOK]), ALU.add).then_inc(bias_ready, 1)

            def staging(freed, copies):
                with loop(gp, TILES // 2, []) as i:
                    for a in range(2):
                        gp.wait_ge(freed, i * 2 + (a + 1))
                        copies(i * 2 + a, a)

            bias_mask("window_mask", 0)
            gp.wait_ge(side_taken, 1)

            def win_copies(p, a):
                gp.tensor_copy(q_st[a][:, :], flat(proj[:, bass.ds(p, 1), :]))
                gp.tensor_copy(k_st[a][:, :], flat(ka_dup[:, bass.ds(p // 4, 1), :]))
                gp.tensor_copy(v_st[a][:, :, 0, :], va_tok[:, :, bass.ds((p // 4) * HD, HD)])
                gp.tensor_copy(v_st[a][:, :, 1, :], va_tok[:, :, bass.ds((p // 4) * HD, HD)]).then_inc(att[0]["staged"], 1)

            staging(att[0]["pv"], win_copies)
            gp.wait_ge(att[0]["pv"], 2 + TILES)

            def idx_copies(p, a):
                gp.tensor_copy(q_st[a][:, :], flat(proj[:, bass.ds(p + T_QI, 1), :])).then_inc(idx_staged, 1)

            staging(idx_dots, idx_copies)
            bias_mask("causal_mask", 1)
            gp.wait_ge(idx_dots, 2 + TILES)

            def sel_copies(p, a):
                gp.tensor_copy(q_st[a][:, :], flat(proj[:, bass.ds(p + T_QB, 1), :]))
                gp.tensor_copy(k_st[a][:, :], flat(kb[:, bass.ds(p, 1), :]))
                gp.tensor_copy(v_st[a][:, :, :, :].rearrange("p h a d -> p h (a d)"),
                               vb_tok[:, :, bass.ds(p * P, P)]).then_inc(att[1]["staged"], 1)

            staging(att[1]["pv"], sel_copies)

        @block.scalar
        def _(act):
            slabs, done, macros, groups, lats = (Count() for _ in range(5))
            act.sem_inc(idx_relu, 2)

            def split(n):
                for _ in range(n):
                    s = slabs.slot(RING)
                    act.wait_ge(raw_landed[s], slabs.turn(RING, 1) * 16)
                    act.wait_ge(slab_used, slabs.value(1))
                    act.activation(w_hi[s][:, :], raw[s][:, :], ACT.Copy).then_inc(hi_ready, 1)
                    slabs.step()

            def product(n):
                done.step(n)
                act.wait_ge(slab_used, done.value(RING))
                s = macros.slot(2)
                return s

            def taken(ins):
                ins.then_inc(acc_taken[macros.slot(2)], 1)
                macros.step()

            vec_src = [
                (0, V_A_NORM, 16, t["a_norm_g"][0]), (0, V_A_SCALE, 32, t["a_scale"][0]), (0, V_KV_NORM, 16, t["kv_norm_g"]),
                (0, V_KV_LAT, 4, t["kv_latent_g"]), (0, V_B_NORM, 16, t["b_norm_g"][0]), (0, V_Q_LAT, 4, t["b_q_latent_g"][0]),
                (0, V_NORM_ATTN, 16, t["norm_attn_2"][0]), (0, V_C, 16, t["c_2"][0]), (0, V_KV_NORM2, 2, t["kv_norm_2"][0]),
                (0, V_KN, 1, t["k_norm_g"][0:NOPE]), (0, V_QN, 1, t["b_q_norm_g"][0, 0:NOPE]),
                (1, 0, 96, t["b_mod_2"][0]), (1, 96, 16, t["norm_ffn_2"][0]), (1, 112, 16, t["norm_final_2"])]
            n_vec = 0
            for r, at, n, v in vec_src:
                act.dma_start(rows[r][at:at + n, :], v.rearrange("(r c) -> r c", c=P)).then_inc(vec_in, 16)
                n_vec += 1
            taps = t["conv_w_2"][0].rearrange("w (r c) -> (w r) c", c=P)
            act.dma_start(rows[2][:, :], taps[0:P, :]).then_inc(vec_in, 16)
            act.dma_start(rows[3][0:3 * KF - P, :], taps[P:3 * KF, :]).then_inc(vec_in, 16)
            act.dma_start(rows[3][3 * KF - P:4 * KF - P, :], t["conv_b_2"][0].rearrange("(r c) -> r c", c=P)).then_inc(vec_in, 16)
            n_vec += 3
            for row, swapped, g in ((V_KR, V_KRS, t["k_norm_g"]), (V_QR, V_QRS, t["b_q_norm_g"][0])):
                for rep in range(2):
                    act.dma_start(rows[0][row:row + 1, rep * ROPE:(rep + 1) * ROPE], g[NOPE:QK].unsqueeze(0)).then_inc(vec_in, 16)
                    for half in range(2):
                        lo = rep * ROPE + half * (ROPE // 2)
                        frm = NOPE + (1 - half) * (ROPE // 2)
                        act.dma_start(rows[0][swapped:swapped + 1, lo:lo + ROPE // 2],
                                      g[frm:frm + ROPE // 2].unsqueeze(0)).then_inc(vec_in, 16)
                    n_vec += 3
            act.dma_start(rel[:, :], t["rel_bias_2"][:, :]).then_inc(rel_in, 16)
            act.dma_start(pos[:, :], t["positions"][0:1, :].broadcast_to([ROPE, TOK])).then_inc(pos_in, 16)
            assert n_vec == N_VEC
            split(RING)

            def squares(first=False):
                for m in range(4):
                    if first:
                        act.wait_ge(x_ready, m + 1)
                    else:
                        taken_by = macros.total() - 4 + m
                        act.wait_ge(acc_taken[taken_by % 2], taken_by // 2 + 2)
                    if m >= 2:
                        act.wait_ge(sq_summed, groups.value(-1))
                    act.activation(tmp[m % 2][:, :, :], xT[:, 4 * m:4 * m + 4, :], ACT.Square).then_inc(sq_ready, 1)
                    groups.step()
                act.wait_ge(sq_summed, groups.value())
                act.activation(rms_std[:, :], rms_sum, ACT.Sqrt, bias=eps[:, :], scale=1.0 / D).then_inc(std_ready, 1)

            norms = Count()

            def h_split(shift=None):
                for m in range(4):
                    norms.step()
                    act.wait_ge(norm_ready, norms.value())
                    for n in range(4 if shift is not None else 1):
                        if shift is None:
                            last = act.activation(h_hi[:, 4 * m:4 * m + 4, :], tmp[m % 2][:, :, :], ACT.Copy)
                        else:
                            last = act.activation(h_hi[:, 4 * m + n, :], tmp[m % 2][:, n, :], ACT.Identity,
                                                  bias=mod[:, shift, 4 * m + n:4 * m + n + 1])
                    last.then_inc(h_hi_ready, 1)

            act.wait_ge(vec_ready, 1)
            act.activation(silu_c[:, :], vec[:, V_C:V_C + KD], ACT.Silu).then_inc(csilu_ready, 1)
            squares(first=True)
            h_split()
            act.wait_ge(line_ready, 1)
            act.dma_start(bias_lines[:, :, :], lines[:, :].unsqueeze(1).broadcast_to([2 * HEADS, P, SC])).then_inc(bias_out, 16)
            act.wait_ge(angle_ready, 1)
            act.activation(sin[:, :], angle[:, 0, :], ACT.Sin)
            act.activation(cos[:, :], angle[:, 1, :], ACT.Sin).then_inc(trig_ready, 1)

            pools = Count()
            with loop(act, GROUPS, [(slabs, 56), (done, 56), (macros, 10), (pools, 2)]) as g:
                def pooled_hi(q):
                    pools.step()
                    act.wait_ge(pool_ready, pools.value())
                    act.activation(pool_hi[:, 4 * q:4 * q + 4, :], tmp[q][:, :, :], ACT.Copy).then_inc(pool_hi_ready, 1)

                def y_split(q):
                    act.wait_ge(acc_taken[macros.slot(2)], macros.turn(2, 2))
                    macros.step()
                    act.activation(y_hi[:, 4 * q:4 * q + 4, :], tmp[q][:, :, :], ACT.Copy).then_inc(y_hi_ready, 1)

                done.step(16)
                macros.step(2)
                split(12)
                pooled_hi(0)
                split(8)
                pooled_hi(1)
                split(4)
                for q in range(2):
                    s = product(8)
                    taken(act.activation(gate_a[:, 4 * q:4 * q + 4, :], acc[s][:, :, :], ACT.Silu))
                    split(8 if q == 0 else 4)
                split(2)
                y_split(0)
                split(4)
                y_split(1)
                split(14)
                done.step(24)
                macros.step(4)

            squares()
            h_split()

            def latent(n_slabs, k, a, b):
                s = product(n_slabs)
                act.activation(b[:, 0:k, :], acc[s][:, 0:k, :], ACT.Square).then_inc(lat_sq, 1)
                taken(act.activation(a[:, 0:k, :], acc[s][:, 0:k, :], ACT.Copy))
                lats.step()

            def latent_split(a, hi, k):
                act.wait_ge(lat_stat, lats.value())
                act.activation(rms_std[:, :], lat_sum, ACT.Sqrt, bias=eps[:, :], scale=1.0 / (k * P)).then_inc(lat_std, 1)
                act.wait_ge(lat_norm, lats.value())
                act.activation(hi[:, :, :], a[:, 0:k, :], ACT.Copy).then_inc(lat_hi_ready, 1)

            split(8)
            latent(8, 4, kq[0], kq[1])
            split(1)
            s = product(1)
            act.activation(kr_sq[:, :], acc[s][0:ROPE, 0, :], ACT.Square)
            act.activation(kr_swap[0:32, :], acc[s][32:64, 0, :], ACT.Copy)
            act.activation(kr_swap[32:64, :], acc[s][0:32, 0, :], ACT.Copy).then_inc(kr_ready, 1)
            macros.step()
            h_split()
            latent_split(kq[0], c_hi, 4)
            split(8)
            act.wait_ge(lat_lo_ready, 1)
            latent(8, 4, kq[0], kq[1])
            latent_split(kq[0], q_hi, 4)
            with loop(act, 2, [(slabs, 16), (done, 16), (macros, 2)]) as i:
                for m in range(2):
                    split(8)
                    s = product(8)
                    taken(act.activation(gate_b[:, bass.ds(i * 8 + m * 4, 4), :], acc[s][:, :, :], ACT.Silu))

            pairs = Count()

            def m_stage(slot):
                skv = product(2)
                macros.step()
                act.activation(vs[slot][:, :, :], acc[skv][:, 2:4, :], ACT.Copy)
                act.activation(tmp[0][:, 0:2, :], acc[skv][:, 0:2, :], ACT.Square)
                sq = product(2)
                macros.step()
                act.activation(tmp[0][:, 2:4, :], acc[sq][:, 0:2, :], ACT.Square)
                act.activation(qr_sq[:, :, :], acc[sq][0:ROPE, 2:4, :], ACT.Square)
                act.wait_ge(m_qk, pairs.value(1))
                act.activation(qr_swap[0:32, :, :], acc[sq][32:64, 2:4, :], ACT.Copy)
                act.activation(qr_swap[32:64, :, :], acc[sq][0:32, 2:4, :], ACT.Copy).then_inc(m_sq, 1)
                pairs.step()

            def m_root():
                act.wait_ge(m_stat, pairs.value())
                act.activation(tmp[1][:, :, :], sums[:, :, :].rearrange("p a (b n) -> p (a b) n", b=2), ACT.Sqrt,
                               bias=eps[:, :], scale=1.0 / QK).then_inc(m_std, 1)

            heads = Count()

            def m_soft():
                heads.step()
                act.wait_ge(m_max_ready, heads.value())
                for half, (lo, hi) in enumerate(((0, P), (P, SC))):
                    for a in range(2):
                        last = act.activation(m_prob[:, a, lo:hi], m_prob[:, a, lo:hi], ACT.Exp, bias=m_neg[:, half, a:a + 1],
                                              accum_out=m_sum[:, half, a:a + 1])
                last.then_inc(m_exp, 1)

            def m_rest(p):
                act.wait_ge(m_turned, heads.value())
                act.activation(m_probT[:, :, :], side[:, :, 0:SC], ACT.Copy).then_inc(m_turned_in, 1)
                act.wait_ge(m_out_ready, heads.value(1))
                act.activation(h_hi[:, bass.ds(p * 2, 2), :], m_out[:, :, :], ACT.Copy).then_inc(m_mix_hi, 1)

            split(4)
            m_stage(0)
            m_root()
            with loop(act, 3, [(slabs, 8), (done, 8), (macros, 4), (pairs, 2), (heads, 2)]) as i:
                for a in range(2):
                    split(4)
                    m_stage(1 - a)
                    m_soft()
                    m_root()
                    m_rest(i * 2 + a)
            split(4)
            m_stage(1)
            m_soft()
            m_root()
            m_rest(6)
            m_soft()
            m_rest(7)
            with loop(act, 2, [(slabs, 16), (done, 16), (macros, 2)]) as i:
                split(16)
                done.step(16)
                macros.step(2)

            def bias_load(n):
                act.dma_start(bias[:, :, :], bass.AP(tensor=bias_lines, offset=n * HEADS * P * SC + P - 1,
                                                     ap=[[SC - 1, P], [P * SC, HEADS], [1, TOK]])).then_inc(bias_in, 16)

            squares()
            act.wait_ge(bias_out, 16)
            bias_load(0)
            act.dma_start(sinks[:, :], t["attn_sinks_2"][0:1, :].broadcast_to([P, HEADS])).then_inc(sinks_in, 16)
            h_split(0)
            with loop(act, 3, [(slabs, 16), (done, 16), (macros, 2)]) as i:
                for m in range(2):
                    split(8)
                    s = product(8)
                    taken(act.activation(proj[:, bass.ds(i * 8 + m * 4, 4), :], acc[s][:, :, :], ACT.Copy))
            split(8)
            s = product(8)
            taken(act.activation(proj[:, 24:28, :], acc[s][:, :, :], ACT.Copy))
            split(2)
            s = product(2)
            taken(act.activation(kiwi[:, :], acc[s][0:KW, 0, :], ACT.Copy))
            act.activation(tmp[0][:, 0:2, :], proj[:, T_C:T_C + 2, :], ACT.Square).then_inc(lat_sq, 1)
            lats.step()
            latent_split(tmp[1], lat_hi, 2)
            split(2)
            done.step(2)
            act.wait_ge(slab_used, done.value(RING))
            for n in range(2):
                s = macros.slot(2)
                taken(act.activation(kb[:, 4 * n:4 * n + 4, :], acc[s][:, :, :], ACT.Copy))
            split(2)
            done.step(2)
            act.wait_ge(slab_used, done.value(RING))
            for n in range(2):
                s = macros.slot(2)
                taken(act.activation(vb_tok[:, n, :], flat(acc[s][:, :, :]), ACT.Copy))

            def attention(kind):
                sm = att[kind]
                soft, rest = Count(), Count()

                def exps(a):
                    soft.step()
                    act.wait_ge(sm["max"], soft.value())
                    for half, (lo, hi) in enumerate(((0, P), (P, SC))):
                        for e in range(2):
                            last = act.activation(prob[a][:, e, lo:hi], prob[a][:, e, lo:hi], ACT.Exp,
                                                  bias=a_neg[a][:, half, e:e + 1], accum_out=a_sum[a][:, half, e:e + 1])
                    if kind == 0:
                        last = act.activation(a_exp[a][:, :, :], a_gap[a][:, :, :], ACT.Exp)
                    last.then_inc(sm["exp"], 1)

                def outs(p):
                    rest.step()
                    act.wait_ge(sm["turned"], rest.value())
                    act.activation(probT[:, :, :], side[:, :, 0:SC], ACT.Copy).then_inc(sm["turned_in"], 1)
                    act.wait_ge(sm["pv"], rest.value(2))
                    act.activation(h_hi[:, bass.ds(p + kind * TILES, 1), :].rearrange("p a t -> p (a t)"),
                                   rms_sum, ACT.Copy).then_inc(sm["mix_hi"], 1)

                exps(0)
                with loop(act, TILES // 2 - 1, [(soft, 2), (rest, 2)]) as i:
                    for a in range(2):
                        exps(1 - a)
                        outs(i * 2 + a)
                exps(1)
                outs(TILES - 2)
                outs(TILES - 1)

            attention(0)
            bias_load(1)
            relus = Count()
            with loop(act, TILES // 2, [(relus, 2)]) as i:
                for a in range(2):
                    relus.step()
                    act.wait_ge(idx_dots, relus.value(2))
                    act.wait_ge(idx_added, relus.value())
                    act.activation(prob[a][:, :, :], acc_banks[a][:, :, 0:SC], ACT.Relu).then_inc(idx_relu, 1)
            attention(1)
            with loop(act, 2, [(slabs, 16), (done, 16), (macros, 2)]) as i:
                split(16)
                done.step(16)
                macros.step(2)
            squares()
            h_split(3)
            def ff_u():
                act.wait_ge(acc_taken[macros.slot(2)], macros.turn(2, 2))
                macros.step()
                act.activation(conv_silu[:, :, :], conv[:, :, :], ACT.Silu).then_inc(conv_silu_ready, 1)

            def ff_g(a):
                act.wait_ge(acc_taken[macros.slot(2)], macros.turn(2, 2))
                macros.step()
                act.activation(f_hi[a][:, :, :], f_raw[:, :, :], ACT.Copy).then_inc(f_hi_ready, 1)

            split(8)
            ff_u()
            split(8)
            ff_g(0)
            with loop(act, FBLOCKS // 2, [(slabs, 48), (macros, 12)]) as i:
                for a in range(2):
                    split(8)
                    ff_u()
                    split(8)
                    ff_g(1 - a)
                    split(8)
                    macros.step(4)
            split(8 - RING)
            macros.step(4)
            squares()
            for m in range(4):
                act.wait_ge(fin_turned, m + 1)
                if m >= 2:
                    act.wait_ge(y_stored[m % 2], 16)
                act.activation(y_tok[m % 2][:, :, :], acc_banks[m % 2], ACT.Copy).then_inc(y_copied, 1)

        @block.vector
        def _(dve):
            slabs, done, macros, norms, lats, steps = (Count() for _ in range(6))
            dve.sem_inc(lo_ready, RING)
            for s in acc_taken:
                dve.sem_inc(s, 1)
            for s in (mod_ready, m_qk, m_out_ready):
                dve.sem_inc(s, 1)
            dve.sem_inc(idx_added, 2)
            for kind in range(2):
                dve.sem_inc(att[kind]["mix_lo"], 1)

            def link(ins):
                steps.step()
                ins.then_inc(dve_step, 1)
                dve.wait_ge(dve_step, steps.value())

            def split(n):
                for _ in range(n):
                    s = slabs.slot(RING)
                    dve.wait_ge(hi_ready, slabs.value(1))
                    dve.tensor_tensor(w_lo[s][:, :], raw[s][:, :], f32(w_hi[s][:, :]), ALU.subtract).then_inc(lo_ready, 1)
                    slabs.step()

            def product(n):
                done.step(n)
                dve.wait_ge(slab_used, done.value(RING))
                return macros.slot(2)

            def taken(ins):
                ins.then_inc(acc_taken[macros.slot(2)], 1)
                macros.step()

            def col(c, n=1, rows=P):
                return vec[0:rows, c:c + n]

            link(dve.memset(ones[:, :], 1.0))
            dve.memset(eps[:, :], EPS).then_inc(const_set, 1)

            dve.wait_ge(vec_turned, 1)
            dve.tensor_copy(vec[:, :], side[:, 0, 0:V_ROWS]).then_inc(vec_ready, 1)
            for m in range(4):
                dve.wait_ge(x_turned, m + 1)
                dve.tensor_copy(xT[:, 4 * m:4 * m + 4, :], acc[m % 2][:, :, :]).then_inc(x_ready, 1)
            dve.wait_ge(line_sum, 1)
            dve.tensor_copy(lines[:, :], side[0:2 * HEADS, 1, 0:SC]).then_inc(line_ready, 1)
            split(RING)

            def norm(gain, shift=None, root=True):
                if root:
                    norms.step()
                    dve.wait_ge(std_ready, norms.value())
                    link(dve.reciprocal(rms_inv[:, :], rms_std[:, :]))

                def scaled(m):
                    if m >= 2:
                        dve.wait_ge(h_lo_ready, first + m - 1)
                    for n in range(4):
                        last = dve.scalar_tensor_tensor(tmp[m % 2][:, n, :], xT[:, 4 * m + n, :], gain(4 * m + n),
                                                        rms_inv[:, :], ALU.mult, ALU.mult)
                    last.then_inc(norm_ready, 1)

                def low(m):
                    h_lows.step()
                    dve.wait_ge(h_hi_ready, h_lows.value())
                    hi = h_hi[:, 4 * m:4 * m + 4, :]
                    if shift is None:
                        last = dve.tensor_tensor(h_lo[:, 4 * m:4 * m + 4, :], tmp[m % 2][:, :, :], f32(hi), ALU.subtract)
                    else:
                        for n in range(4):
                            c = 4 * m + n
                            last = dve.scalar_tensor_tensor(h_lo[:, c, :], tmp[m % 2][:, n, :], mod[:, shift, c:c + 1],
                                                            f32(h_hi[:, c, :]), ALU.add, ALU.subtract)
                    last.then_inc(h_lo_ready, 1)

                first = h_lows.total()
                scaled(0)
                scaled(1)
                low(0)
                scaled(2)
                low(1)
                scaled(3)
                low(2)
                low(3)

            h_lows = Count()
            norm(lambda c: col(V_A_NORM + c))

            dve.wait_ge(pos_in, 16)
            dve.wait_ge(table_in, 16)
            link(dve.tensor_copy(angle[:, 2, :], pos[:, :]))
            link(dve.tensor_scalar(angle[:, 2, :], angle[:, 2, :], tab("inv_freq", rows=ROPE), None, ALU.mult))
            for n, quarter in ((0, 0.0), (1, 0.25)):
                link(dve.tensor_scalar(angle[:, 3, :], angle[:, 2, :], float(1 / (2 * np.pi)), quarter, ALU.mult, ALU.add))
                link(dve.tensor_scalar(angle[:, 3, :], angle[:, 3, :], ROUND, None, ALU.add))
                link(dve.tensor_scalar(angle[:, 3, :], angle[:, 3, :], -ROUND, None, ALU.add))
                link(dve.scalar_tensor_tensor(angle[:, n, :], angle[:, 3, :], -TWO_PI_A, angle[:, 2, :], ALU.mult, ALU.add))
                link(dve.scalar_tensor_tensor(angle[:, n, :], angle[:, 3, :], -TWO_PI_B, angle[:, n, :], ALU.mult, ALU.add))
                link(dve.scalar_tensor_tensor(angle[:, n, :], angle[:, 3, :], -TWO_PI_C, angle[:, n, :], ALU.mult, ALU.add))
                link(dve.tensor_scalar(angle[:, n, :], angle[:, n, :], quarter * float(2 * np.pi), None, ALU.add))
                last = dve.tensor_scalar(angle[:, n, :], angle[:, n, :], PI_CLAMP, -PI_CLAMP, ALU.min, ALU.max)
                if n == 0:
                    link(last)
            last.then_inc(angle_ready, 1)
            dve.wait_ge(trig_ready, 1)
            link(dve.tensor_scalar(sin[:, :], sin[:, :], tab("rope_sign", rows=ROPE), None, ALU.mult))
            link(dve.memset(csum[:, :, 0:PAD], 0.0))

            def add_product(n_slabs, m, scale=None):
                s = product(n_slabs)
                if scale is None:
                    taken(dve.tensor_tensor(xT[:, bass.ds(m, 4), :], acc[s][:, :, :], xT[:, bass.ds(m, 4), :], ALU.add))
                else:
                    for n in range(4):
                        x = flat(xT[:, bass.ds(m + n, 1), :])
                        last = dve.scalar_tensor_tensor(x, acc[s][:, n, :], mod[:, scale, bass.ds(m + n, 1)], x, ALU.mult, ALU.add)
                    taken(last)

            mods = Count()

            def take_mod(v):
                mods.step()
                dve.wait_ge(mod_summed, mods.value())
                m = flat(mod[:, bass.ds(v, 1), :])
                dve.tensor_tensor(m, side[:, 1, 0:KD], vec[:, bass.ds(v * KD + V_BMOD, KD)], ALU.add).then_inc(mod_ready, 1)

            pools, ys = Count(), Count()
            with loop(dve, GROUPS, [(slabs, 56), (done, 56), (macros, 10), (pools, 2), (ys, 2), (steps, 6), (mods, 1)]) as g:
                window = (g * g * g + g * 5) // 3 + 2

                def pool(q):
                    s = product(8)
                    for n in range(4):
                        last = dve.tensor_tensor_scan(csum[:, n, PAD:PAD + TOK], ones[:, :], acc[s][:, n, :], 0.0, ALU.mult, ALU.add)
                    link(last)
                    link(dve.tensor_tensor(tmp[q][:, :, :], csum[:, :, PAD:PAD + TOK],
                                           csum[:, :, bass.ds(PAD - window, TOK)], ALU.subtract))
                    rc0 = cols["rcount"][0]
                    rcount = table[:, bass.ds(g * PAD + rc0, PAD)].unsqueeze(1).broadcast_to([P, 4, PAD])
                    link(dve.tensor_tensor(first16[:, :, :], tmp[q][:, :, 0:PAD], rcount, ALU.mult))
                    dve.tensor_tensor(first16[:, :, :], first16[:, :, :], acc[s][:, :, 0:PAD], ALU.subtract)
                    dve.scalar_tensor_tensor(tmp[q][:, :, :], tmp[q][:, :, :], table[:, bass.ds(g + cols["rwindow"][0], 1)],
                                             acc[s][:, :, :], ALU.mult, ALU.subtract).then_inc(acc_taken[s], 1)
                    dve.wait_ge(acc_taken[s], macros.turn(2, 2))
                    macros.step()
                    dve.tensor_copy(tmp[q][:, :, 0:PAD], first16[:, :, :]).then_inc(pool_ready, 1)

                def pooled_lo(q):
                    pools.step()
                    dve.wait_ge(pool_hi_ready, pools.value())
                    c = slice(4 * q, 4 * q + 4)
                    dve.tensor_tensor(pool_lo[:, c, :], tmp[q][:, :, :], f32(pool_hi[:, c, :]), ALU.subtract).then_inc(pool_lo_ready, 1)

                def gate(q):
                    s = product(4)
                    for n in range(4):
                        last = dve.scalar_tensor_tensor(tmp[q][:, n, :], acc[s][:, n, :], vec[:, bass.ds(g * 8 + (V_A_SCALE + 4 * q + n), 1)],
                                                        gate_a[:, 4 * q + n, :], ALU.mult, ALU.mult)
                    taken(last)

                def y_low(q):
                    ys.step()
                    dve.wait_ge(y_hi_ready, ys.value())
                    c = slice(4 * q, 4 * q + 4)
                    dve.tensor_tensor(y_lo[:, c, :], tmp[q][:, :, :], f32(y_hi[:, c, :]), ALU.subtract).then_inc(y_lo_ready, 1)

                split(8)
                pool(0)
                split(4)
                pooled_lo(0)
                split(4)
                pool(1)
                split(4)
                pooled_lo(1)
                split(4 + 8 + 4)
                for q in range(2):
                    done.step(8)
                    dve.wait_ge(acc_taken[macros.slot(2)], macros.turn(2, 2))
                    macros.step()
                gate(0)
                split(2)
                y_low(0)
                split(2)
                gate(1)
                split(2)
                y_low(1)
                split(2)
                for m in range(4):
                    add_product(4, 4 * m)
                    if m < 3:
                        split(4)
                take_mod(g)

            norm(lambda c: col(V_KV_NORM + c))

            def latent(a, k, gain, hi, lo, src=None):
                lats.step()
                dve.wait_ge(lat_std, lats.value())
                link(dve.reciprocal(rms_inv[:, :], rms_std[:, :]))
                for n in range(k):
                    last = dve.scalar_tensor_tensor(a[:, n, :], (src or (lambda n: a[:, n, :]))(n), col(gain + n),
                                                    rms_inv[:, :], ALU.mult, ALU.mult)
                last.then_inc(lat_norm, 1)
                dve.wait_ge(lat_hi_ready, lats.value())
                dve.tensor_tensor(lo[:, :, :], a[:, 0:k, :], f32(hi[:, :, :]), ALU.subtract).then_inc(lat_lo_ready, 1)

            split(8)
            done.step(8)
            macros.step()
            split(1)
            s = product(1)
            dve.wait_ge(kr_ready, 1)
            taken(dve.scalar_tensor_tensor(kr_rot[:, :], acc[s][0:ROPE, 0, :], col(V_KR, rows=ROPE), cos[:, :], ALU.mult, ALU.mult))
            norm(lambda c: col(V_B_NORM + c), root=False)
            latent(kq[0], 4, V_KV_LAT, c_hi, c_lo)
            link(dve.scalar_tensor_tensor(kr_swap[:, :], kr_swap[:, :], col(V_KRS, rows=ROPE), sin[:, :], ALU.mult, ALU.mult))
            dve.tensor_tensor(kr_rot[:, :], kr_rot[:, :], kr_swap[:, :], ALU.add).then_inc(kr_done, 1)
            split(8)
            done.step(8)
            macros.step()
            latent(kq[0], 4, V_Q_LAT, q_hi, q_lo)
            with loop(dve, 2, [(slabs, 16), (done, 16), (macros, 2)]) as i:
                split(16)
                done.step(16)
                macros.step(2)
            take_mod(4)

            pairs, heads = Count(), Count()
            rope_cos = cos[:, :].unsqueeze(1).broadcast_to([ROPE, 2, TOK])
            rope_sin = sin[:, :].unsqueeze(1).broadcast_to([ROPE, 2, TOK])

            def m_take(slot):
                pairs.step()
                dve.wait_ge(m_sq, pairs.value())
                skv = product(2)
                taken(dve.tensor_scalar(kq[slot][:, 0:2, :], acc[skv][:, 0:2, :], col(V_KN), None, ALU.mult))
                sq = product(2)
                dve.tensor_scalar(kq[slot][:, 2:4, :], acc[sq][:, 0:2, :], col(V_QN), None, ALU.mult)
                taken(dve.scalar_tensor_tensor(qr[slot][:, :, :], acc[sq][0:ROPE, 2:4, :], col(V_QR, rows=ROPE), rope_cos, ALU.mult, ALU.mult))

            def m_rotate(slot):
                dve.wait_ge(m_std, pairs.value())
                inv = tmp[1]
                link(dve.scalar_tensor_tensor(qr_swap[:, :, :], qr_swap[:, :, :], col(V_QRS, rows=ROPE), rope_sin, ALU.mult, ALU.mult))
                link(dve.reciprocal(inv[:, :, :], inv[:, :, :]))
                dve.tensor_tensor(kq[slot][:, :, :], kq[slot][:, :, :], inv[:, :, :], ALU.mult)
                dve.tensor_tensor(kr[slot][:, :, :], kr_rot[:, :].unsqueeze(1).broadcast_to([ROPE, 2, TOK]), inv[0:ROPE, 0:2, :], ALU.mult)
                link(dve.tensor_tensor(qr[slot][:, :, :], qr[slot][:, :, :], qr_swap[:, :, :], ALU.add))
                dve.tensor_tensor(qr[slot][:, :, :], qr[slot][:, :, :], inv[0:ROPE, 2:4, :], ALU.mult).then_inc(m_qk, 1)

            def row_max(mx, pr):
                dve.tensor_reduce(mx[:, 0, :], pr[:, :, 0:P], AX.X, ALU.max)
                link(dve.tensor_reduce(mx[:, 1, :], pr[:, :, P:SC], AX.X, ALU.max))

            def scale_rows(pr, inv):
                dve.tensor_tensor(pr[:, :, 0:P], pr[:, :, 0:P], inv[:, 0, :].unsqueeze(2).broadcast_to([P, 2, P]), ALU.mult)
                return dve.tensor_tensor(pr[:, :, P:SC], pr[:, :, P:SC], inv[:, 1, :].unsqueeze(2).broadcast_to([P, 2, TOK]), ALU.mult)

            def m_soft():
                heads.step()
                dve.wait_ge(m_score, heads.value())
                link(dve.scalar_tensor_tensor(m_prob[:, :, :], side[:, :, 0:SC], QK ** -0.5,
                                              tab("chunk_mask").unsqueeze(1).broadcast_to([P, 2, SC]), ALU.mult, ALU.add))
                row_max(m_max, m_prob)
                dve.tensor_scalar(m_neg[:, :, :], m_max[:, :, :], -1.0, None, ALU.mult).then_inc(m_max_ready, 1)
                dve.wait_ge(m_exp, heads.value())
                link(dve.reciprocal(m_inv[:, :, :], m_sum[:, :, :]))
                scale_rows(m_prob, m_inv).then_inc(m_prob_ready, 1)

            def m_gate(p):
                dve.wait_ge(m_pv, heads.value())
                dve.tensor_tensor(flat(m_out[:, :, :]), side[:, 0, :], flat(gate_b[:, bass.ds(p * 2, 2), :]), ALU.mult)\
                    .then_inc(m_out_ready, 1)
                dve.wait_ge(m_mix_hi, heads.value())
                dve.tensor_tensor(h_lo[:, bass.ds(p * 2, 2), :], m_out[:, :, :], f32(h_hi[:, bass.ds(p * 2, 2), :]), ALU.subtract)\
                    .then_inc(mix_lo, 1)

            split(4)
            m_take(0)
            m_rotate(0)
            with loop(dve, 3, [(slabs, 8), (done, 8), (macros, 4), (pairs, 2), (heads, 2), (steps, 12)]) as i:
                for a in range(2):
                    split(4)
                    m_take(1 - a)
                    m_soft()
                    m_rotate(1 - a)
                    m_gate(i * 2 + a)
            split(4)
            m_take(1)
            m_soft()
            m_rotate(1)
            m_gate(6)
            m_soft()
            m_gate(7)
            with loop(dve, 2, [(slabs, 16), (done, 16), (macros, 2)]) as i:
                for m in range(2):
                    split(8)
                    add_product(8, i * 8 + 4 * m)
            take_mod(5)

            dve.wait_ge(mod_ready, 7)
            dve.scalar_tensor_tensor(gain2[:, :], mod[:, 4, :], 1.0, col(V_NORM_FFN, KD), ALU.add, ALU.mult)
            link(dve.scalar_tensor_tensor(gain1[:, :], mod[:, 1, :], 1.0, col(V_NORM_ATTN, KD), ALU.add, ALU.mult))
            norm(lambda c: gain1[:, c:c + 1], shift=0)
            with loop(dve, 3, [(slabs, 16), (done, 16), (macros, 2)]) as i:
                split(16)
                done.step(16)
                macros.step(2)
            split(8 + 2)
            done.step(8 + 2)
            macros.step(2)
            latent(tmp[1], 2, V_KV_NORM2, lat_hi, lat_lo, src=lambda n: proj[:, T_C + n, :])
            dve.wait_ge(side_done, 1)
            dve.tensor_copy(flat(ka_dup[:, :, :]), side[:, 0, :])
            dve.tensor_copy(flat(va_tok[:, :, :]), side[:, 1, 0:TOK])
            dve.tensor_copy(ki_dup[:, :], side[:, 1, TOK:2 * TOK])
            wi = sums[:, 0, 0:2 * P].rearrange("p (h n) -> p h n", h=2)
            dve.tensor_scalar(wi_tok[:, :, :], wi[:, :, HD:KW], IDX_SCALE, None, ALU.mult).then_inc(side_taken, 1)
            split(4)
            done.step(4)
            macros.step(4)
            dve.wait_ge(sinks_in, 16)

            def attention(kind):
                sm = att[kind]
                soft, rest = Count(), Count()

                def softmax(p, a):
                    soft.step()
                    dve.wait_ge(sm["score"], soft.value())
                    pr = prob[a]
                    dve.scalar_tensor_tensor(pr[:, :, 0:P], acc_banks[a][:, :, 0:P], HD ** -0.5, bias[:, bass.ds(p * 2, 2), P:TOK],
                                             ALU.mult, ALU.add)
                    link(dve.scalar_tensor_tensor(pr[:, :, P:SC], acc_banks[a][:, :, P:SC], HD ** -0.5, bias[:, bass.ds(p * 2, 2), :],
                                                  ALU.mult, ALU.add))
                    if kind == 1:
                        link(dve.tensor_tensor(pr[:, :, :], pr[:, :, :], sel[:, :].unsqueeze(1).broadcast_to([P, 2, SC]), ALU.add))
                    row_max(a_max[a], pr)
                    if kind == 0:
                        sink = sinks[:, bass.ds(p * 2, 2)].unsqueeze(1).broadcast_to([P, 2, 2])
                        link(dve.tensor_tensor(a_max[a][:, :, :], a_max[a][:, :, :], sink, ALU.max))
                        dve.tensor_tensor(a_gap[a][:, :, :], sink, a_max[a][:, :, :], ALU.subtract)
                    dve.tensor_scalar(a_neg[a][:, :, :], a_max[a][:, :, :], -1.0, None, ALU.mult).then_inc(sm["max"], 1)

                def scale(a):
                    rest.step()
                    dve.wait_ge(sm["exp"], rest.value())
                    if kind == 0:
                        link(dve.tensor_tensor(a_sum[a][:, :, :], a_sum[a][:, :, :], a_exp[a][:, :, :], ALU.add))
                    link(dve.reciprocal(a_inv[:, :, :], a_sum[a][:, :, :]))
                    scale_rows(prob[a], a_inv).then_inc(sm["prob"], 1)

                def mix_low(p):
                    dve.wait_ge(sm["mix_hi"], rest.value())
                    c = bass.ds(p + kind * TILES, 1)
                    dve.tensor_tensor(flat(h_lo[:, c, :]), rms_sum, f32(flat(h_hi[:, c, :])), ALU.subtract).then_inc(sm["mix_lo"], 1)

                dve.wait_ge(bias_ready, kind + 1)
                softmax(0, 0)
                with loop(dve, TILES // 2 - 1, [(soft, 2), (rest, 2), (steps, 10 - 2 * kind)]) as i:
                    for a in range(2):
                        softmax(i * 2 + (a + 1), 1 - a)
                        scale(a)
                        mix_low(i * 2 + a)
                softmax(TILES - 1, 1)
                scale(0)
                mix_low(TILES - 2)
                scale(1)
                mix_low(TILES - 1)

            attention(0)

            dve.tensor_copy(idx[:, 0:P], tab("causal_mask", P, TOK))
            link(dve.tensor_copy(idx[:, P:SC], tab("causal_mask")))
            halves = ((0, slice(0, P)), (1, slice(P, SC)))
            relus = Count()
            with loop(dve, TILES // 2, [(relus, 2), (steps, 2)]) as i:
                for a in range(2):
                    relus.step()
                    dve.wait_ge(idx_relu, relus.value(2))
                    dve.wait_ge(idx_added, relus.value(1))
                    for e in range(2):
                        for half, c in halves:
                            last = dve.scalar_tensor_tensor(idx[:, c], prob[a][:, e, c], flat(wi_tok[:, half:half + 1, bass.ds(i * 4 + (2 * a + e), 1)]),
                                                            idx[:, c], ALU.mult, ALU.add)
                        if e == 0:
                            link(last)
                    last.then_inc(idx_added, 1)
            dve.wait_ge(idx_added, 2 + TILES)
            link(dve.tensor_copy(idx_work[:, :], idx[:, :]))
            for r in range(TOPK // 8):
                for half, c in halves:
                    last = dve.max(top8[:, half, :], idx_work[:, c])
                link(last)
                if r < TOPK // 8 - 1:
                    for half, c in halves:
                        last = dve.match_replace(idx_work[:, c], top8[:, half, :], idx_work[:, c], -3e38)
                    link(last)
            cum, equal = prob[0][:, 0, :], prob[0][:, 1, :]
            for half, c in halves:
                thr = top8[:, half, 7:8]
                dve.tensor_scalar(idx_work[:, c], idx[:, c], thr, None, ALU.is_gt)
                last = dve.tensor_scalar(equal[:, c], idx[:, c], thr, None, ALU.is_equal)
            link(last)
            for half, c in halves:
                dve.tensor_reduce(quota[:, half:half + 1], idx_work[:, c], AX.X, ALU.add)
                last = dve.tensor_tensor_scan(cum[:, c], ones[:, 0:c.stop - c.start], equal[:, c], 0.0, ALU.mult, ALU.add)
            link(last)
            link(dve.tensor_scalar(quota[:, :], quota[:, :], -1.0, float(TOPK), ALU.mult, ALU.add))
            for half, c in halves:
                last = dve.scalar_tensor_tensor(sel[:, c], cum[:, c], quota[:, half:half + 1], equal[:, c], ALU.is_le, ALU.mult)
            link(last)
            link(dve.tensor_tensor(sel[:, :], sel[:, :], idx_work[:, :], ALU.add))
            link(dve.tensor_scalar(sel[:, :], sel[:, :], -1.0, -NEG, ALU.add, ALU.mult))
            attention(1)

            with loop(dve, 2, [(slabs, 16), (done, 16), (macros, 2)]) as i:
                for m in range(2):
                    split(8)
                    add_product(8, i * 8 + 4 * m, scale=2)
            norm(lambda c: gain2[:, c:c + 1], shift=3)

            ffs = Count()

            def ff_conv(i):
                ffs.step()
                s = product(8)

                def tap(w, n):
                    return vec[:, bass.ds(i * 4 + (V_CONV + w * KF + n), 1)]

                for n in range(4):
                    last = dve.tensor_scalar(conv[:, n, :], acc[s][:, n, :], tap(2, n), vec[:, bass.ds(i * 4 + (V_CONVB + n), 1)], ALU.mult, ALU.add)
                link(last)
                for n in range(4):
                    last = dve.scalar_tensor_tensor(conv[:, n, 1:TOK], acc[s][:, n, 0:TOK - 1], tap(1, n), conv[:, n, 1:TOK], ALU.mult, ALU.add)
                link(last)
                for n in range(4):
                    last = dve.scalar_tensor_tensor(conv[:, n, 2:TOK], acc[s][:, n, 0:TOK - 2], tap(0, n), conv[:, n, 2:TOK], ALU.mult, ALU.add)
                taken(last)

            def ff_gate(a):
                s = product(8)
                dve.wait_ge(conv_silu_ready, ffs.value())
                taken(dve.tensor_tensor(f_raw[:, :, :], acc[s][:, :, :], conv_silu[:, :, :], ALU.mult))

            def ff_low(a):
                dve.wait_ge(f_hi_ready, ffs.value())
                dve.tensor_tensor(f_lo[a][:, :, :], f_raw[:, :, :], f32(f_hi[a][:, :, :]), ALU.subtract).then_inc(f_lo_ready, 1)

            split(8)
            ff_conv(0)
            split(8)
            ff_gate(0)
            ff_low(0)
            with loop(dve, FBLOCKS // 2, [(slabs, 48), (done, 48), (macros, 12), (ffs, 2), (steps, 4)]) as i:
                for a in range(2):
                    split(8)
                    ff_conv(i * 2 + (a + 1))
                    split(8)
                    ff_gate(1 - a)
                    ff_low(1 - a)
                    for m in range(4):
                        split(2)
                        add_product(2, 4 * m, scale=5)
            for m in range(4):
                if m < 2:
                    split(2)
                add_product(2, 4 * m, scale=5)

            norms.step()
            dve.wait_ge(std_ready, norms.value())
            link(dve.reciprocal(rms_inv[:, :], rms_std[:, :]))
            for m in range(4):
                if m >= 2:
                    dve.wait_ge(fin_turned, m - 1)
                for n in range(4):
                    last = dve.scalar_tensor_tensor(tmp[m % 2][:, n, :], xT[:, 4 * m + n, :], col(V_NORM_FIN + 4 * m + n),
                                                    rms_inv[:, :], ALU.mult, ALU.mult)
                last.then_inc(fin_ready, 1)

        @block.tensor
        def _(pe):
            slabs, macros, groups, h_groups, lats = (Count() for _ in range(5))
            pe.sem_inc(slab_used, RING)
            pe.sem_inc(idx_dots, 2)
            for kind in range(2):
                pe.sem_inc(att[kind]["pv"], 2)
            ident = tab("ident")

            def mm(o, lhsT, rhs, start=False, stop=False):
                return pe.matmul(o, lhsT, rhs, start=start, stop=stop, skip_group_check=True)

            def w_slot(k, n):
                s = slabs.slot(RING)
                hi = w_hi[s][:, 0:k * n].rearrange("p (k n) -> p k n", k=k)
                lo = w_lo[s][:, 0:k * n].rearrange("p (k n) -> p k n", k=k)
                pe.wait_ge(lo_ready, slabs.value(RING + 1))
                return hi, lo

            def set_free():
                s = macros.slot(2)
                pe.wait_ge(acc_taken[s], macros.turn(2, 1))
                macros.step()
                return s

            def gemm(n_slabs, x_hi, x_lo, tiles, k=SLAB_K, n=SLAB_N, before=None):
                a = acc[set_free()]
                for s in range(n_slabs):
                    hi, lo = w_slot(k, n)
                    if before:
                        before(s)
                    for i, (c0, rows) in enumerate(tiles):
                        o = a[0:rows, i, :]
                        for kk in range(k):
                            x = s * k + kk
                            first = s == 0 and kk == 0 and i % 2 == 0
                            end = s == n_slabs - 1 and kk == k - 1 and (i % 2 == 1 or i == len(tiles) - 1)
                            mm(o, hi[:, kk, c0:c0 + rows], x_hi[:, x, :], start=first)
                            mm(o, hi[:, kk, c0:c0 + rows], x_lo[:, x, :])
                            last = mm(o, lo[:, kk, c0:c0 + rows], x_hi[:, x, :], stop=end)
                    last.then_inc(slab_used, 1)
                    slabs.step()

            four = [(i * P, P) for i in range(4)]

            def sum_squares(k_tiles, o, x, first, end):
                for n in range(k_tiles):
                    last = mm(o, ones[:, 0:P], x[:, n, :], start=first and n == 0, stop=end and n == k_tiles - 1)
                return last

            def norm_sums():
                for m in range(4):
                    groups.step()
                    pe.wait_ge(sq_ready, groups.value())
                    sum_squares(4, rms_sum, tmp[m % 2], m == 0, m == 3).then_inc(sq_summed, 1)

            def h_ready(base):
                def before(s):
                    if s % 2 == 0:
                        pe.wait_ge(h_lo_ready, base + s // 2 + 1)
                return before

            pe.wait_ge(table_in, 16)
            pe.wait_ge(vec_in, 16 * N_VEC)
            for r, n in enumerate((P, P, P, V_ROWS - 3 * P)):
                last = pe.transpose(side[:, 0, r * P:r * P + n], rows[r][0:n, :], ident[0:n, 0:n])
            last.then_inc(vec_turned, 1)
            pe.wait_ge(rel_in, 16)
            mm(side[0:2 * HEADS, 1, 0:SC], rel[:, :], tab("onehot", rows=BUCKETS), start=True, stop=True).then_inc(line_sum, 1)
            pe.wait_ge(x_in, 16)
            for m in range(4):
                if m >= 2:
                    pe.wait_ge(x_ready, m - 1)
                for n in range(4):
                    for half in range(HALVES):
                        c = (4 * m + n) * P
                        last = pe.transpose(acc[m % 2][:, n, half * P:(half + 1) * P], x_tok[:, half, c:c + P], ident)
                last.then_inc(x_turned, 1)
            pe.wait_ge(const_set, 1)
            norm_sums()

            mods = Count()

            def mod_sum():
                mods.step()
                pe.wait_ge(mod_step, mods.value() * (4 * KD - 2))
                for n in range(KD):
                    last = mm(side[:, 1, n:n + 1], mod_acc[:, n * P:(n + 1) * P], ones[:, 0:1], start=n == 0, stop=n == KD - 1)
                last.then_inc(mod_summed, 1)

            pe.wait_ge(line_ready, 1)
            pools, ys = Count(), Count()
            with loop(pe, GROUPS, [(slabs, 56), (macros, 10), (pools, 2), (ys, 2), (mods, 1)]) as g:
                for m in range(4):
                    gemm(8, h_hi, h_lo, four, before=h_ready(0))

                def pooled(s):
                    if s % 2 == 0:
                        pe.wait_ge(pool_lo_ready, pools.value(s // 2 + 1))

                def gated(s):
                    if s % 2 == 0:
                        pe.wait_ge(y_lo_ready, ys.value(s // 2 + 1))

                for m in range(2):
                    gemm(4, pool_hi, pool_lo, four, before=pooled)
                pools.step(2)
                for m in range(4):
                    gemm(4, y_hi, y_lo, four, before=gated)
                ys.step(2)
                mod_sum()

            norm_sums()
            gemm(8, h_hi, h_lo, four, before=h_ready(4))
            gemm(1, h_hi, h_lo, [(0, ROPE)], k=KD, n=ROPE)

            def latent_sum(x, k):
                lats.step()
                pe.wait_ge(lat_sq, lats.value())
                sum_squares(k, lat_sum, x, True, True).then_inc(lat_stat, 1)

            latent_sum(kq[1], 4)
            gemm(8, h_hi, h_lo, four, before=h_ready(8))
            latent_sum(kq[1], 4)
            with loop(pe, 2, [(slabs, 16), (macros, 2)]) as i:
                for m in range(2):
                    gemm(8, h_hi, h_lo, four)
            mod_sum()

            pairs, heads = Count(), Count()
            pe.wait_ge(lat_lo_ready, 2)
            pe.wait_ge(kr_done, 1)
            pe.wait_ge(mod_ready, 6)

            def m_gemm():
                a = acc[set_free()]
                for s in range(2):
                    hi, lo = w_slot(2, 512)
                    for e in range(2):
                        for kk in range(2):
                            x = 2 * s + kk
                            c = slice(e * (NOPE + VD), e * (NOPE + VD) + NOPE)
                            mm(a[:, e, :], hi[:, kk, c], c_hi[:, x, :], start=s == 0 and kk == 0 and e == 0)
                            mm(a[:, e, :], hi[:, kk, c], c_lo[:, x, :])
                            mm(a[:, e, :], lo[:, kk, c], c_hi[:, x, :], stop=s == 1 and kk == 1 and e == 1)
                    for half in range(HALVES):
                        o = a[:, 2 + half, :].rearrange("p (e d) -> p e d", e=2)
                        tok = slice(half * P, (half + 1) * P)
                        for kk in range(2):
                            x = 2 * s + kk
                            v_hi = hi[:, kk, :].rearrange("p (e d) -> p e d", e=2)[:, :, NOPE:NOPE + VD]
                            v_lo = lo[:, kk, :].rearrange("p (e d) -> p e d", e=2)[:, :, NOPE:NOPE + VD]
                            mm(o, c_hi[:, x, tok], v_hi, start=s == 0 and kk == 0 and half == 0)
                            mm(o, c_hi[:, x, tok], v_lo)
                            last = mm(o, c_lo[:, x, tok], v_hi, stop=s == 1 and kk == 1 and half == 1)
                    last.then_inc(slab_used, 1)
                    slabs.step()
                gemm(2, q_hi, q_lo, [(0, NOPE), (QK, NOPE), (NOPE, ROPE), (QK + NOPE, ROPE)], n=2 * QK)

            def m_sums():
                pairs.step()
                pe.wait_ge(m_sq, pairs.value())
                for e in range(4):
                    o = sums[:, e // 2, (e % 2) * TOK:(e % 2 + 1) * TOK]
                    mm(o, ones[:, 0:P], tmp[0][:, e, :], start=e % 2 == 0)
                    last = mm(o, ones[0:ROPE, 0:P], kr_sq[:, :] if e < 2 else qr_sq[:, e - 2, :], stop=e % 2 == 1)
                last.then_inc(m_stat, 1)

            def m_scores(slot):
                heads.step()
                pe.wait_ge(m_qk, heads.value(1))
                pe.wait_ge(m_out_ready, heads.value())
                for e in range(2):
                    for half, (lo, n) in enumerate(((0, P), (P, TOK))):
                        tok = slice(half * P, (half + 1) * P)
                        o = side[:, e, lo:lo + n]
                        mm(o, kq[slot][:, 2 + e, tok], kq[slot][:, e, 0:n], start=half == 0)
                        last = mm(o, qr[slot][:, e, tok], kr[slot][:, e, 0:n], stop=half == 1)
                last.then_inc(m_score, 1)

            def turn(pr):
                for e in range(2):
                    for b in range(3):
                        c = slice(b * P, (b + 1) * P)
                        last = pe.transpose(side[:, e, c], pr[:, e, c], ident)
                return last

            def weigh(o, v0, v1, pT, start, stop):
                mm(o[:, 0:P], v0, pT[:, 0:P], start=start)
                mm(o[:, P:TOK], v0, pT[:, P:2 * P])
                return mm(o[:, P:TOK], v1, pT[:, 2 * P:SC], stop=stop)

            def m_output(slot):
                pe.wait_ge(m_prob_ready, heads.value())
                turn(m_prob).then_inc(m_turned, 1)
                pe.wait_ge(m_turned_in, heads.value())
                for e in range(2):
                    d = slice(e * VD, (e + 1) * VD)
                    last = weigh(side[:, 0, e * TOK:(e + 1) * TOK], vs[slot][:, 0, d], vs[slot][:, 1, d], m_probT[:, e, :], e == 0, e == 1)
                last.then_inc(m_pv, 1)

            m_gemm()
            m_sums()
            with loop(pe, 3, [(slabs, 8), (macros, 4), (pairs, 2), (heads, 2)]) as i:
                for a in range(2):
                    m_gemm()
                    m_scores(a)
                    m_sums()
                    m_output(a)
            m_gemm()
            m_scores(0)
            m_sums()
            m_output(0)
            m_scores(1)
            m_output(1)
            pe.wait_ge(mix_lo, PAIRS)
            with loop(pe, 2, [(slabs, 16), (macros, 2)]) as i:
                for m in range(2):
                    gemm(8, h_hi, h_lo, four)
            mod_sum()

            norm_sums()
            with loop(pe, 3, [(slabs, 16), (macros, 2)]) as i:
                for m in range(2):
                    gemm(8, h_hi, h_lo, four, before=h_ready(12))
            gemm(8, h_hi, h_lo, four)
            gemm(2, h_hi, h_lo, [(0, KW)], k=8, n=KW)
            latent_sum(tmp[0], 2)
            pe.wait_ge(acc_taken[(macros.total() - 1) % 2], (macros.total() - 1) // 2 + 2)
            pe.wait_ge(mod_ready, 7)
            for n in range(2):
                mm(side[:, 0, n * TOK:(n + 1) * TOK], tab(f"dup{n}"), proj[:, T_KA, :], start=n == 0, stop=n == 1)
            mm(side[:, 1, TOK:2 * TOK], tab("dup0", rows=HD), kiwi[0:HD, :], start=True, stop=True)
            pe.wait_ge(std_ready, 3)
            for half in range(HALVES):
                tok = slice(half * P, (half + 1) * P)
                pe.transpose(side[:, 1, half * P:(half + 1) * P], proj[:, T_VA, tok], ident)
                last = pe.transpose(sums[:, 0, half * P:half * P + KW], kiwi[:, tok], ident[0:KW, 0:KW])
            last.then_inc(side_done, 1)

            pe.wait_ge(lat_lo_ready, 3)
            sets = [set_free(), set_free()]
            for r in range(2):
                hi, lo = w_slot(1, SLAB)
                for i in range(TILES):
                    o = acc[sets[i // 4]][:, i % 4, :]
                    c = slice(i * P, (i + 1) * P)
                    mm(o, hi[:, 0, c], lat_hi[:, r, :], start=r == 0 and i % 2 == 0)
                    mm(o, hi[:, 0, c], lat_lo[:, r, :])
                    last = mm(o, lo[:, 0, c], lat_hi[:, r, :], stop=r == 1 and i % 2 == 1)
                last.then_inc(slab_used, 1)
                slabs.step()
            sets = [set_free(), set_free()]
            for r in range(2):
                hi, lo = w_slot(1, SLAB)
                for half in range(HALVES):
                    tok = slice(half * P, (half + 1) * P)
                    for b in range(2):
                        o = acc_banks[sets[half]][:, b, :]
                        c = slice(b * 512, (b + 1) * 512)
                        mm(o, lat_hi[:, r, tok], hi[:, 0, c], start=r == 0)
                        mm(o, lat_hi[:, r, tok], lo[:, 0, c])
                        last = mm(o, lat_lo[:, r, tok], hi[:, 0, c], stop=r == 1)
                last.then_inc(slab_used, 1)
                slabs.step()
            for s in range(2):
                pe.wait_ge(acc_taken[s], (macros.total() + 1 - s) // 2 + 1)
            pe.wait_ge(side_taken, 1)

            def tile_scores(a):
                for e in range(2):
                    d = slice(e * HD, (e + 1) * HD)
                    mm(acc_banks[a][:, e, 0:P], q_st[a][d, 0:P], k_st[a][d, 0:P], start=True)
                    last = mm(acc_banks[a][:, e, P:SC], q_st[a][d, P:TOK], k_st[a][d, :], stop=True)
                return last

            def attention(kind):
                sm = att[kind]
                front, back = Count(), Count()

                def scores(a):
                    front.step()
                    pe.wait_ge(sm["staged"], front.value())
                    tile_scores(a).then_inc(sm["score"], 1)

                def output(a):
                    back.step()
                    pe.wait_ge(sm["prob"], back.value())
                    turn(prob[a]).then_inc(sm["turned"], 1)
                    pe.wait_ge(sm["turned_in"], back.value())
                    pe.wait_ge(sm["mix_lo"], back.value())
                    for e in range(2):
                        last = weigh(sums[e * HD:(e + 1) * HD, 0, 0:TOK], v_st[a][:, 0, e, :], v_st[a][:, 1, e, :], probT[:, e, :], True, True)
                    last.then_inc(sm["pv"], 1)

                scores(0)
                with loop(pe, TILES // 2 - 1, [(front, 2), (back, 2)]) as i:
                    for a in range(2):
                        scores(1 - a)
                        output(a)
                scores(1)
                output(0)
                output(1)

            attention(0)
            dots = Count()
            with loop(pe, TILES // 2, [(dots, 2)]) as i:
                for a in range(2):
                    dots.step()
                    pe.wait_ge(idx_staged, dots.value())
                    pe.wait_ge(idx_relu, dots.value())
                    for e in range(2):
                        d = slice(e * HD, (e + 1) * HD)
                        mm(acc_banks[a][:, e, 0:P], q_st[a][d, 0:P], ki_dup[d, 0:P], start=True)
                        last = mm(acc_banks[a][:, e, P:SC], q_st[a][d, P:TOK], ki_dup[d, :], stop=True)
                    last.then_inc(idx_dots, 1)
            pe.wait_ge(idx_relu, 2 + TILES)
            attention(1)
            for kind in range(2):
                pe.wait_ge(att[kind]["mix_lo"], 1 + TILES)
            with loop(pe, 2, [(slabs, 16), (macros, 2)]) as i:
                for m in range(2):
                    gemm(8, h_hi, h_lo, four)

            norm_sums()
            ffs = Count()

            def ff_up(before=None):
                for m in range(2):
                    gemm(8, h_hi, h_lo, four, before=before)

            def ff_down(a):
                ffs.step()
                pe.wait_ge(f_lo_ready, ffs.value())
                for m in range(4):
                    gemm(2, f_hi[a], f_lo[a], four)

            ff_up(h_ready(16))
            with loop(pe, FBLOCKS // 2, [(slabs, 48), (macros, 12), (ffs, 2)]) as i:
                for a in range(2):
                    ff_up()
                    ff_down(a)
            ff_down(0)

            norm_sums()
            for s in range(2):
                pe.wait_ge(acc_taken[s], (macros.total() + 1 - s) // 2 + 1)
            for m in range(4):
                pe.wait_ge(fin_ready, m + 1)
                if m >= 2:
                    pe.wait_ge(y_copied, m - 1)
                for half in range(HALVES):
                    for n in range(4):
                        last = pe.transpose(acc_banks[m % 2][:, half, n * P:(n + 1) * P], tmp[m % 2][:, n, half * P:(half + 1) * P], ident)
                last.then_inc(fin_turned, 1)


INPUTS = ("x", "positions", "a_norm_g", "a_w_in", "a_w_group", "a_scale", "a_w_out", "kv_norm_g", "kv_w_a", "kv_latent_g",
          "kv_w_b", "k_norm_g", "b_norm_g", "b_w_in", "b_q_latent_g", "b_w_q_b", "b_q_norm_g", "b_w_out", "c_2",
          "w_mod_2", "b_mod_2", "norm_attn_2", "w_in_2", "attn_sinks_2", "kv_norm_2", "w_uk_2", "w_uv_2", "rel_bias_2",
          "w_out_2", "norm_ffn_2", "w_up_2", "conv_w_2", "conv_b_2", "w_down_2", "norm_final_2")


def kernel(**inputs):
    import concourse.bacc as bacc
    from concourse.bass_utils import run_bass_kernel_spmd

    nc = bacc.Bacc("TRN2", target_bir_lowering=False, num_devices=1)
    consts, cols = constants()
    arrays = {name: np.ascontiguousarray(inputs[name]) for name in INPUTS}
    arrays["consts"] = consts
    dram = {name: nc.dram_tensor(f"in_{name}", a.shape, mybir.dt.from_np(a.dtype), kind="ExternalInput").ap()
            for name, a in arrays.items()}
    out = nc.dram_tensor("out_0", (1, TOK, D), F32, kind="ExternalOutput").ap()
    two_block_kernel(nc, dram, out, cols)
    ran = run_bass_kernel_spmd(nc, [{f"in_{name}": a for name, a in arrays.items()}], core_ids=[0])
    return ran.results[0]["out_0"]
```

```python
from contextlib import ExitStack, contextmanager

import numpy as np

import concourse.bass as bass
from concourse import mybir

F32 = mybir.dt.float32
F32R = mybir.dt.float32r
I32 = mybir.dt.int32
ALU = mybir.AluOpType
ACT = mybir.ActivationFunctionType
AX = mybir.AxisListType

P = 128
TOK = 256
HALVES = TOK // P
D = 2048
KD = D // P
EPS = 1e-6
NEG = -1e30

POOL_WINDOWS = (2, 4, 8, 16)
GROUPS = len(POOL_WINDOWS)
W_A = 2 * D
G_A = W_A // GROUPS
PAD = max(POOL_WINDOWS)
HEADS = 16
NOPE, ROPE, VD, LORA = 128, 64, 128, 512
QK = NOPE + ROPE
CHUNK = 64
PAIRS = HEADS // 2

HD = 64
TILES = HEADS * HD // P
RANK = 256
TOPK = 64
WINDOW = 128
BUCKETS = 32
DFF = 5632
KF = DFF // P
FBLOCKS = DFF // 512
IDX_SCALE = HD ** -0.5 * HEADS ** -0.5
COL_QA, COL_KA, COL_VA, COL_QB, COL_C, COL_QI, COL_KW = 0, 1024, 1152, 1280, 2304, 2560, 3584
KW = HD + HEADS
T_KA, T_VA, T_QB, T_C, T_QI = COL_KA // P, COL_VA // P, COL_QB // P, COL_C // P, COL_QI // P
PROJ = COL_KW // P
N_VEC = 29

RING = 4
AHEAD = 3
SLAB_K = 2
SLAB_N = 512
SLAB = SLAB_K * SLAB_N
SC = P + TOK

V_A_NORM, V_A_SCALE, V_KV_NORM, V_KV_LAT, V_B_NORM, V_Q_LAT = 0, 16, 48, 64, 68, 84
V_NORM_ATTN, V_C, V_KV_NORM2, V_KN, V_QN, V_KR, V_QR, V_KRS, V_QRS = 88, 104, 120, 122, 123, 124, 125, 126, 127
V_BMOD, V_NORM_FFN, V_NORM_FIN, V_CONV, V_CONVB = 128, 224, 240, 256, 256 + 3 * KF
V_ROWS = V_CONVB + KF

TWO_PI_A = 6.28125
TWO_PI_B = float(np.float32(np.round((2 * np.pi - TWO_PI_A) * 2 ** 21) / 2 ** 21))
TWO_PI_C = float(2 * np.pi - TWO_PI_A - TWO_PI_B)
ROUND = 1.5 * 2 ** 23
PI_CLAMP = 3.1415925


def constants():
    q = np.arange(P)[:, None]
    parts = {}
    parts["ident"] = np.eye(P)
    parts["dup0"] = (np.arange(P)[:, None] == np.arange(P)[None] % HD)
    parts["dup1"] = (np.arange(P)[:, None] == HD + np.arange(P)[None] % HD)
    k0, k1 = np.arange(P)[None], np.arange(TOK)[None]
    parts["chunk_mask"] = np.concatenate([np.where(k0 // CHUNK <= q // CHUNK, 0, NEG),
                                          np.where(k1 // CHUNK <= (q + P) // CHUNK, 0, NEG)], 1)
    dist = q + P - k1
    parts["window_mask"] = np.where((dist >= 0) & (dist < WINDOW), 0, NEG)
    parts["causal_mask"] = np.where(dist >= 0, 0, NEG)
    t = np.arange(PAD)
    parts["rcount"] = np.tile(np.concatenate([1 / np.minimum(t + 1, w) for w in POOL_WINDOWS])[None], (P, 1))
    parts["rwindow"] = np.tile(np.array([1 / w for w in POOL_WINDOWS])[None], (P, 1))
    parts["inv_freq"] = np.tile(np.float32(10000.0) ** (-np.arange(0, ROPE, 2, dtype=np.float32) / np.float32(ROPE)), 4)[:, None]
    parts["rope_sign"] = np.where(np.arange(P) % ROPE < ROPE // 2, -1.0, 1.0)[:, None]
    parts["head_rows"] = q // ROPE == np.arange(2)[None]
    n = TOK - 1 - np.arange(SC)
    exact = BUCKETS // 2
    large = exact + (np.log(np.maximum(n, 1).astype(np.float32) / exact) / np.log(128 / exact) * (BUCKETS - exact)).astype(np.int32)
    bucket = np.where(n < exact, n, np.minimum(large, BUCKETS - 1))
    onehot = np.zeros((P, SC))
    onehot[bucket[n >= 0], np.arange(SC)[n >= 0]] = 1
    parts["onehot"] = onehot
    cols, at = {}, 0
    for name, a in parts.items():
        cols[name] = (at, at + a.shape[1])
        at += a.shape[1]
    return np.ascontiguousarray(np.concatenate([a.astype(np.float32) for a in parts.values()], 1)), cols


class Count:

    def __init__(self):
        self.base, self.k, self.i, self.per = 0, 0, None, 0

    def enter(self, i, per):
        self.i, self.per, self.base, self.k = i, per, self.base + self.k, 0

    def leave(self, n):
        assert self.k == self.per, (self.k, self.per)
        self.base, self.k, self.i = self.base + n * self.per, 0, None

    def step(self, n=1):
        self.k += n

    def value(self, add=0):
        v = self.base + self.k + add
        return v if self.i is None else self.i * self.per + v

    def total(self):
        assert self.i is None
        return self.base + self.k

    def slot(self, ring):
        assert self.i is None or self.per % ring == 0
        return (self.base + self.k) % ring

    def turn(self, ring, add=0):
        v = (self.base + self.k) // ring + add
        return v if self.i is None else self.i * (self.per // ring) + v


@contextmanager
def loop(eng, n, counts):
    with eng.Fori(0, n) as i:
        for c, per in counts:
            c.enter(i, per)
        yield i
        for c, _ in counts:
            c.leave(n)


def two_block_kernel(nc, t, out, cols):
    fixed = ExitStack()
    with fixed:
        def sb(name, shape, dt=F32, scope=fixed):
            return scope.enter_context(nc.sbuf_tensor(name, shape, dt))

        def sem(name):
            return fixed.enter_context(nc.semaphore(name))

        xT = sb("xT", [P, KD, TOK])
        h_hi = sb("h_hi", [P, KD, TOK], F32R)
        h_lo = sb("h_lo", [P, KD, TOK], F32R)
        raw = [sb(f"raw{s}", [P, SLAB]) for s in range(RING)]
        w_hi = [sb(f"w_hi{s}", [P, SLAB], F32R) for s in range(RING)]
        w_lo = [sb(f"w_lo{s}", [P, SLAB], F32R) for s in range(RING)]
        tmp = [sb(f"tmp{s}", [P, 4, TOK]) for s in range(2)]
        table = sb("table", [P, t["consts"].shape[1]])
        vec = sb("vec", [P, V_ROWS])
        ones = sb("ones", [P, TOK])
        eps = sb("eps", [P, 1])
        rms_std = sb("rms_std", [P, TOK])
        rms_inv = sb("rms_inv", [P, TOK])
        lat_inv = sb("lat_inv", [P, TOK])
        mod = sb("mod", [P, 6, KD])
        gain1 = sb("gain1", [P, KD])
        gain2 = sb("gain2", [P, KD])
        silu_c = sb("silu_c", [P, KD])
        rel = sb("rel", [BUCKETS, 2 * HEADS])
        lines = sb("lines", [2 * HEADS, SC])
        cos = sb("cos", [P, TOK])
        sin = sb("sin", [P, TOK])

        def tab(name, a=0, b=None, rows=P):
            lo, hi = cols[name]
            return table[0:rows, lo + a:(hi if b is None else lo + b)]

        acc = [fixed.enter_context(nc.psum_tensor(f"acc{s}", [P, 4, TOK], F32)) for s in range(2)]
        sums = fixed.enter_context(nc.psum_tensor("sums", [P, 2, 512], F32))
        side = fixed.enter_context(nc.psum_tensor("side", [P, 2, 512], F32))
        rms_sum, lat_sum = sums[:, 0, 0:TOK], sums[:, 1, 0:TOK]
        acc_banks = [a[:, :, :].rearrange("p (b j) t -> p b (j t)", b=2) for a in acc]
        bias_lines = nc.dram_tensor("bias_lines", [2 * HEADS, P, SC], F32)

        mod_scope = ExitStack()
        mod_raw = [sb(f"mod_raw{s}", [P, 1024], F32, mod_scope) for s in range(2)]
        mod_acc = sb("mod_acc", [P, D], F32, mod_scope)

        with ExitStack() as scope:
            x_tok = sb("x_tok", [P, HALVES, D], F32, scope)
            rows = [sb(f"vec_rows{s}", [P, P], F32, scope) for s in range(4)]
        with ExitStack() as scope:
            pool_hi = sb("pool_hi", [P, 8, TOK], F32R, scope)
            pool_lo = sb("pool_lo", [P, 8, TOK], F32R, scope)
            y_hi = sb("y_hi", [P, 8, TOK], F32R, scope)
            y_lo = sb("y_lo", [P, 8, TOK], F32R, scope)
            gate_a = sb("gate_a", [P, 8, TOK], F32, scope)
            csum = sb("csum", [P, 4, PAD + TOK], F32, scope)
            first16 = sb("first16", [P, 4, PAD], F32, scope)
        with ExitStack() as scope:
            hk_hi = sb("hk_hi", [P, KD, TOK], F32R, scope)
            hk_lo = sb("hk_lo", [P, KD, TOK], F32R, scope)
        with ExitStack() as scope:
            c_hi = sb("c_hi", [P, 4, TOK], F32R, scope)
            c_lo = sb("c_lo", [P, 4, TOK], F32R, scope)
            q_hi = sb("q_hi", [P, 4, TOK], F32R, scope)
            q_lo = sb("q_lo", [P, 4, TOK], F32R, scope)
            gate_b = sb("gate_b", [P, HEADS, TOK], F32, scope)
            kr_raw = sb("kr_raw", [P, TOK], F32, scope)
            kr_swap = sb("kr_swap", [P, TOK], F32, scope)
            kr_rot = sb("kr_rot", [P, TOK], F32, scope)
            kr_sq = sb("kr_sq", [ROPE, TOK], F32, scope)
            kq = [sb(f"kq{s}", [P, 4, TOK], F32, scope) for s in range(2)]
            qr = [sb(f"qr{s}", [P, TOK], F32, scope) for s in range(2)]
            vs = [sb(f"vs{s}", [P, HALVES, 2 * VD], F32, scope) for s in range(2)]
            qr_swap = sb("qr_swap", [P, TOK], F32, scope)
            qr_sq = sb("qr_sq", [P, TOK], F32, scope)
            m_root = sb("m_root", [P, 8], F32, scope)
            m_rinv = sb("m_rinv", [P, 8], F32, scope)
            m_diag = sb("m_diag", [P, 2 * TOK], F32, scope)
            m_kinv = sb("m_kinv", [P, 2 * TOK], F32, scope)
            m_prob = sb("m_prob", [P, 2, SC], F32, scope)
            m_probT = sb("m_probT", [P, 2, SC], F32, scope)
            m_out = sb("m_out", [P, 2, TOK], F32, scope)
            m_max = sb("m_max", [P, 2, 2], F32, scope)
            m_neg = sb("m_neg", [P, 2, 2], F32, scope)
            m_sum = sb("m_sum", [P, 2, 2], F32, scope)
            m_inv = sb("m_inv", [P, 2, 2], F32, scope)
            pos = sb("pos", [P, TOK], I32, scope)
            angle = [v[:, n, :] for v in vs for n in range(2)]
        mod_scope.close()
        with ExitStack() as scope:
            proj = sb("proj", [P, PROJ, TOK], F32, scope)
            bias = sb("bias", [P, HEADS, TOK], F32, scope)
            kiwi = sb("kiwi", [KW, TOK], F32, scope)
            ki_dup = sb("ki_dup", [P, TOK], F32, scope)
            ka_dup = sb("ka_dup", [P, 2, TOK], F32, scope)
            va_tok = sb("va_tok", [P, HALVES, 2 * HD], F32, scope)
            wi_tok = sb("wi_tok", [P, HALVES, HEADS], F32, scope)
            lat_hi = sb("lat_hi", [P, 2, TOK], F32R, scope)
            lat_lo = sb("lat_lo", [P, 2, TOK], F32R, scope)
            kb = sb("kb", [P, TILES, TOK], F32, scope)
            vb_tok = sb("vb_tok", [P, HALVES, HEADS * HD], F32, scope)
            prob = [sb(f"prob{s}", [P, 2, SC], F32, scope) for s in range(AHEAD)]
            probT = [sb(f"probT{s}", [P, 2, SC], F32, scope) for s in range(2)]
            sinks = sb("sinks", [P, HEADS], F32, scope)
            idx, idx_work = probT[0][:, 0, :], probT[1][:, 0, :]
            sel = sb("sel", [P, SC], F32, scope)
            top8 = sb("top8", [P, HALVES, 8], F32, scope)
            quota = sb("quota", [P, HALVES], F32, scope)
            a_max = [sb(f"a_max{s}", [P, 2, 2], F32, scope) for s in range(AHEAD)]
            a_neg = [sb(f"a_neg{s}", [P, 2, 2], F32, scope) for s in range(AHEAD)]
            a_sum = [sb(f"a_sum{s}", [P, 2, 2], F32, scope) for s in range(AHEAD)]
            a_gap = [sb(f"a_gap{s}", [P, 2, 2], F32, scope) for s in range(AHEAD)]
            a_exp = [sb(f"a_exp{s}", [P, 2, 2], F32, scope) for s in range(AHEAD)]
            a_inv = [sb(f"a_inv{s}", [P, 2, 2], F32, scope) for s in range(AHEAD)]
        with ExitStack() as scope:
            conv = sb("conv", [P, 4, TOK], F32, scope)
            conv_silu = sb("conv_silu", [P, 4, TOK], F32, scope)
            f_raw = sb("f_raw", [P, 4, TOK], F32, scope)
            f_hi = [sb(f"f_hi{s}", [P, 4, TOK], F32R, scope) for s in range(2)]
            f_lo = [sb(f"f_lo{s}", [P, 4, TOK], F32R, scope) for s in range(2)]
            y_tok = [sb(f"y_tok{s}", [P, HALVES, 512], F32, scope) for s in range(2)]

        raw_landed = [sem(f"raw_landed{s}") for s in range(RING)]
        hi_ready = sem("hi_ready")
        lo_ready = sem("lo_ready")
        slab_used = sem("slab_used")
        acc_taken = [sem(f"acc_taken{s}") for s in range(2)]
        ident_in, table_in, vec_in, x_in, rel_in, pos_in, bias_in, bias_out, sinks_in = map(sem, (
            "ident_in", "table_in", "vec_in", "x_in", "rel_in", "pos_in", "bias_in", "bias_out", "sinks_in"))
        const_set, x_turned, vec_turned, vec_ready, line_sum, line_ready = map(sem, (
            "const_set", "x_turned", "vec_turned", "vec_ready", "line_sum", "line_ready"))
        x_ready = sem("x_ready")
        sq_ready, sq_summed, std_ready, norm_ready, h_hi_ready, h_lo_ready = map(sem, (
            "sq_ready", "sq_summed", "std_ready", "norm_ready", "h_hi_ready", "h_lo_ready"))
        pool_ready, pool_hi_ready, pool_lo_ready = map(sem, ("pool_ready", "pool_hi_ready", "pool_lo_ready"))
        y_hi_ready, y_lo_ready = map(sem, ("y_hi_ready", "y_lo_ready"))
        csilu_ready, mod_summed, mod_ready = map(sem, ("csilu_ready", "mod_summed", "mod_ready"))
        mod_landed = [sem(f"mod_landed{s}") for s in range(2)]
        lat_sq, lat_stat, lat_std, lat_norm, lat_hi_ready, lat_lo_ready = map(sem, (
            "lat_sq", "lat_stat", "lat_std", "lat_norm", "lat_hi_ready", "lat_lo_ready"))
        angle_ready, trig_ready, kr_ready, kr_done = map(sem, ("angle_ready", "trig_ready", "kr_ready", "kr_done"))
        m_ksq, m_sq, m_swapped, m_folded, gate_ready, m_stat, m_std, m_recip, m_diag_ready, m_spread, m_kinv_ready, m_qk, m_score, m_max_ready, m_exp, m_prob_ready, \
            m_turned, m_turned_in, m_pv, m_out_ready, m_mix_hi, mix_lo = map(sem, (
                "m_ksq", "m_sq", "m_swapped", "m_folded", "gate_ready", "m_stat", "m_std", "m_recip", "m_diag_ready", "m_spread", "m_kinv_ready", "m_qk", "m_score", "m_max_ready",
                "m_exp", "m_prob_ready", "m_turned", "m_turned_in", "m_pv", "m_out_ready", "m_mix_hi", "mix_lo"))
        side_done, side_taken, bias_ready = map(sem, ("side_done", "side_taken", "bias_ready"))
        idx_dots, idx_relu, idx_added = map(sem, ("idx_dots", "idx_relu", "idx_added"))
        att = []
        for kind in ("win", "sel"):
            att.append({n: sem(f"{kind}_{n}") for n in (
                "score", "max", "exp", "inv", "prob", "turned", "turned_in", "pv", "mix_hi", "mix_lo")})
        conv_silu_ready, f_hi_ready, f_lo_ready = map(sem, ("conv_silu_ready", "f_hi_ready", "f_lo_ready"))
        fin_ready, fin_turned = sem("fin_ready"), sem("fin_turned")
        y_stored = [sem(f"y_stored{s}") for s in range(2)]
        y_copied = sem("y_copied")
        dve_step = sem("dve_step")
        mod_started = sem("mod_started")
        mod_step = sem("mod_step")

        def query_parts(tile, split):
            w = tile[:, 0:SLAB_K * 2 * QK].rearrange("p (k n) -> p k n", k=SLAB_K)
            if split:
                return [w[:, :, a:b].rearrange("p k (e c) -> p k e c", e=2) for a, b in ((0, 2 * NOPE), (2 * NOPE, 2 * QK))]
            w = w.rearrange("p k (e c) -> p k e c", e=2)
            return [w[:, :, :, 0:NOPE], w[:, :, :, NOPE:QK]]

        block = fixed.enter_context(nc.Block())

        def f32(ap):
            return ap.bitcast(F32)

        def flat(ap):
            return ap.rearrange("p a b -> p (a b)")

        @block.sync
        def _(sp):
            slabs = Count()

            def load(src, k, n):
                sp.wait_ge(lo_ready, slabs.value(1))
                s = slabs.slot(RING)
                sp.dma_start(raw[s][:, 0:k * n].rearrange("p (k n) -> p k n", k=k),
                             src.rearrange("(k p) n -> p k n", p=P)).then_inc(raw_landed[s], 16)
                slabs.step()

            def stream(w, rows, row0, col0, n=SLAB_N):
                for r in range(0, rows, SLAB_K * P):
                    load(w[bass.ds(row0 + r, SLAB_K * P), bass.ds(col0, n)], SLAB_K, n)

            ident_cols = slice(*cols["ident"])
            assert ident_cols.start == 0
            sp.dma_start(table[:, ident_cols], t["consts"][:, ident_cols]).then_inc(ident_in, 16)
            sp.dma_start(x_tok[:, :, :], t["x"][0].rearrange("(h p) d -> p h d", p=P)).then_inc(x_in, 16)
            taps = t["conv_w_2"][0].rearrange("w (r c) -> (w r) c", c=P)
            sp.dma_start(rows[2][:, :], taps[0:P, :]).then_inc(vec_in, 16)
            sp.dma_start(rows[3][0:3 * KF - P, :], taps[P:3 * KF, :]).then_inc(vec_in, 16)
            sp.dma_start(rows[3][3 * KF - P:4 * KF - P, :], t["conv_b_2"][0].rearrange("(r c) -> r c", c=P)).then_inc(vec_in, 16)
            for row, swapped, g in ((V_KR, V_KRS, t["k_norm_g"]), (V_QR, V_QRS, t["b_q_norm_g"][0])):
                for rep in range(2):
                    sp.dma_start(rows[0][row:row + 1, rep * ROPE:(rep + 1) * ROPE], g[NOPE:QK].unsqueeze(0)).then_inc(vec_in, 16)
                    for half in range(2):
                        lo = rep * ROPE + half * (ROPE // 2)
                        frm = NOPE + (1 - half) * (ROPE // 2)
                        sp.dma_start(rows[0][swapped:swapped + 1, lo:lo + ROPE // 2],
                                     g[frm:frm + ROPE // 2].unsqueeze(0)).then_inc(vec_in, 16)
            sp.dma_start(table[:, P:], t["consts"][:, P:]).then_inc(table_in, 16)
            a_in, a_out = t["a_w_in"][0], t["a_w_out"][0]
            a_group = t["a_w_group"][0].rearrange("g c d -> (g c) d")
            with loop(sp, GROUPS, [(slabs, 56)]) as g:
                for half in range(2):
                    stream(a_in, D, 0, g * G_A + half * SLAB_N)
                for half in range(2):
                    stream(a_in, D, 0, g * G_A + (W_A + half * SLAB_N))
                for half in range(2):
                    stream(a_group, G_A, g * G_A, half * SLAB_N)
                for m in range(4):
                    stream(a_out, G_A, g * G_A, m * SLAB_N)
            stream(t["kv_w_a"], D, 0, 0)
            load(t["kv_w_a"][:, LORA:LORA + ROPE], KD, ROPE)
            stream(t["b_w_in"][0], D, 0, 0)
            with loop(sp, 2, [(slabs, 16)]) as i:
                for m in range(2):
                    stream(t["b_w_in"][0], D, 0, i * 1024 + (m + 1) * SLAB_N)

            def pair(p):
                stream(t["kv_w_b"], LORA, 0, p * 512)
                stream(t["b_w_q_b"][0], LORA, 0, p * 384, 384)

            with loop(sp, PAIRS // 2, [(slabs, 8)]) as i:
                pair(i * 2)
                pair(i * 2 + 1)
            for w in (t["b_w_out"][0],):
                with loop(sp, 2, [(slabs, 16)]) as i:
                    for m in range(2):
                        stream(w, D, 0, i * 1024 + m * SLAB_N)
            w_in = t["w_in_2"][0]
            with loop(sp, 3, [(slabs, 16)]) as i:
                for m in range(2):
                    stream(w_in, D, 0, i * 1024 + m * SLAB_N)
            stream(w_in, D, 0, 6 * SLAB_N)
            for r in range(2):
                load(w_in[r * 1024:(r + 1) * 1024, COL_KW:COL_KW + KW], 8, KW)

            for w in (t["w_uk_2"], t["w_uv_2"]):
                for r in range(RANK // P):
                    sp.wait_ge(lo_ready, slabs.value(1))
                    s = slabs.slot(RING)
                    sp.dma_start(raw[s][:, :].rearrange("p (h d) -> p h d", d=HD),
                                 w[0, :, r * P:(r + 1) * P, :].rearrange("h p d -> p h d")).then_inc(raw_landed[s], 16)
                    slabs.step()
            for r in range(2):
                with loop(sp, 2, [(slabs, 8)]) as i:
                    for m in range(2):
                        stream(t["w_out_2"][0], D // 2, r * (D // 2), i * 1024 + m * SLAB_N)
            up, down = t["w_up_2"][0], t["w_down_2"][0]

            def ff_up(i):
                stream(up, D, 0, i * SLAB_N)
                stream(up, D, 0, i * SLAB_N + DFF)

            def ff_down(i):
                for m in range(4):
                    stream(down, SLAB_N, i * SLAB_N, m * SLAB_N)

            ff_up(0)
            with loop(sp, FBLOCKS // 2, [(slabs, 48)]) as i:
                for a in range(2):
                    ff_up(i * 2 + (a + 1))
                    ff_down(i * 2 + a)
            ff_down(FBLOCKS - 1)
            out_v = out[0].rearrange("(h p) d -> p h d", p=P)
            for m in range(4):
                sp.wait_ge(y_copied, m + 1)
                sp.dma_start(out_v[:, :, m * 512:(m + 1) * 512], y_tok[m % 2][:, :, :]).then_inc(y_stored[m % 2], 16)
            for s in range(2):
                sp.wait_ge(y_stored[s], 32)

        @block.gpsimd
        def _(gp):
            gp.wait_ge(csilu_ready, 1)
            w_mod = t["w_mod_2"][0]
            slabs, steps = Count(), Count()

            def mod_load(v, j):
                s = j % 2
                gp.dma_start(mod_raw[s][:, :], w_mod[(j // 2) * P:(j // 2 + 1) * P, bass.ds(v * D + (j % 2) * 1024, 1024)])\
                    .then_inc(mod_landed[s], 16)

            with loop(gp, 6, [(slabs, 2 * KD), (steps, 4 * KD - 2)]) as v:
                mod_load(v, 0)
                mod_load(v, 1)
                gp.wait_ge(mod_ready, v + 1)
                for j in range(2 * KD):
                    s, k = j % 2, j // 2
                    a = mod_acc[:, s * 1024:(s + 1) * 1024]
                    gp.wait_ge(mod_landed[s], slabs.turn(2, 1) * 16)
                    gp.sem_inc(mod_started, 1)
                    slabs.step()
                    if k == 0:
                        gp.tensor_scalar(a, mod_raw[s][:, :], silu_c[:, 0:1], 1.0, ALU.mult, ALU.mult).then_inc(mod_step, 1)
                        steps.step()
                    else:
                        gp.tensor_scalar(mod_raw[s][:, :], mod_raw[s][:, :], silu_c[:, k:k + 1], 1.0, ALU.mult, ALU.mult)\
                            .then_inc(mod_step, 1)
                        steps.step()
                        gp.wait_ge(mod_step, steps.value())
                        gp.tensor_tensor(a, a, mod_raw[s][:, :], ALU.add).then_inc(mod_step, 1)
                        steps.step()
                    gp.wait_ge(mod_step, steps.value())
                    if j + 2 < 2 * KD:
                        mod_load(v, j + 2)

            def bias_mask(kind, n):
                gp.wait_ge(bias_in, 16 * (n + 1))
                gp.tensor_tensor(bias[:, :, :], bias[:, :, :],
                                 tab(kind).unsqueeze(1).broadcast_to([P, HEADS, TOK]), ALU.add).then_inc(bias_ready, 1)

            def scale(kind):
                for p in range(TILES):
                    gp.wait_ge(att[kind]["inv"], p + 1)
                    pr, inv = prob[p % AHEAD], a_inv[p % AHEAD]
                    for half, (lo, hi) in enumerate(((0, P), (P, SC))):
                        for e in range(2):
                            last = gp.tensor_scalar(pr[:, e, lo:hi], pr[:, e, lo:hi], inv[:, half, e:e + 1], 1.0, ALU.mult, ALU.mult)
                    last.then_inc(att[kind]["prob"], 1)

            bias_mask("window_mask", 0)
            scale(0)
            bias_mask("causal_mask", 1)
            scale(1)

        @block.scalar
        def _(act):
            slabs, done, macros, groups, lats = (Count() for _ in range(5))

            def split(n):
                for _ in range(n):
                    s = slabs.slot(RING)
                    act.wait_ge(raw_landed[s], slabs.turn(RING, 1) * 16)
                    act.wait_ge(slab_used, slabs.value(1))
                    act.activation(w_hi[s][:, :], raw[s][:, :], ACT.Copy).then_inc(hi_ready, 1)
                    slabs.step()

            def split_queries(n):
                for _ in range(n):
                    s = slabs.slot(RING)
                    act.wait_ge(raw_landed[s], slabs.turn(RING, 1) * 16)
                    act.wait_ge(slab_used, slabs.value(1))
                    for o, x in zip(query_parts(w_hi[s], True), query_parts(raw[s], False)):
                        last = act.activation(o, x, ACT.Copy)
                    last.then_inc(hi_ready, 1)
                    slabs.step()

            def product(n):
                done.step(n)
                act.wait_ge(slab_used, done.value(RING))
                s = macros.slot(2)
                return s

            def taken(ins):
                ins.then_inc(acc_taken[macros.slot(2)], 1)
                macros.step()

            vec_src = [
                (0, V_A_NORM, 16, t["a_norm_g"][0]), (0, V_A_SCALE, 32, t["a_scale"][0]), (0, V_KV_NORM, 16, t["kv_norm_g"]),
                (0, V_KV_LAT, 4, t["kv_latent_g"]), (0, V_B_NORM, 16, t["b_norm_g"][0]), (0, V_Q_LAT, 4, t["b_q_latent_g"][0]),
                (0, V_NORM_ATTN, 16, t["norm_attn_2"][0]), (0, V_C, 16, t["c_2"][0]), (0, V_KV_NORM2, 2, t["kv_norm_2"][0]),
                (0, V_KN, 1, t["k_norm_g"][0:NOPE]), (0, V_QN, 1, t["b_q_norm_g"][0, 0:NOPE]),
                (1, 0, 96, t["b_mod_2"][0]), (1, 96, 16, t["norm_ffn_2"][0]), (1, 112, 16, t["norm_final_2"])]
            for r, at, n, v in vec_src:
                act.dma_start(rows[r][at:at + n, :], v.rearrange("(r c) -> r c", c=P)).then_inc(vec_in, 16)
            act.dma_start(rel[:, :], t["rel_bias_2"][:, :]).then_inc(rel_in, 16)
            act.dma_start(pos[:, :], t["positions"][0:1, :].broadcast_to([P, TOK])).then_inc(pos_in, 16)
            def square(m, buffers=tmp):
                if m >= 2:
                    act.wait_ge(sq_summed, groups.value(-1))
                act.activation(buffers[m % 2][:, :, :], xT[:, 4 * m:4 * m + 4, :], ACT.Square).then_inc(sq_ready, 1)
                groups.step()

            def tiles_final(m):
                by = macros.total() - 4 + m
                act.wait_ge(acc_taken[by % 2], by // 2 + 2)

            def root():
                act.wait_ge(sq_summed, groups.value())
                act.activation(rms_std[:, :], rms_sum, ACT.Sqrt, bias=eps[:, :], scale=1.0 / D).then_inc(std_ready, 1)

            def squares(first=False):
                for m in range(4):
                    if first:
                        act.wait_ge(x_ready, m + 1)
                    else:
                        tiles_final(m)
                    square(m)
                if first:
                    split(RING)
                root()

            norms = Count()

            def h_split(shift=None, hi=h_hi):
                for j in range(KD // 2):
                    norms.step()
                    act.wait_ge(norm_ready, norms.value())
                    x = tmp[j // 2 % 2][:, j % 2 * 2:j % 2 * 2 + 2, :]
                    if shift is None:
                        last = act.activation(hi[:, 2 * j:2 * j + 2, :], x, ACT.Copy)
                    else:
                        for n in range(2):
                            c = 2 * j + n
                            last = act.activation(hi[:, c, :], x[:, n, :], ACT.Identity, bias=mod[:, shift, c:c + 1])
                    last.then_inc(h_hi_ready, 1)

            squares(first=True)
            act.wait_ge(vec_ready, 1)
            act.activation(silu_c[:, :], vec[:, V_C:V_C + KD], ACT.Silu).then_inc(csilu_ready, 1)
            h_split()

            pools = Count()
            with loop(act, GROUPS, [(slabs, 56), (done, 56), (macros, 10), (pools, 2)]) as g:
                def pooled_hi(q):
                    pools.step()
                    act.wait_ge(pool_ready, pools.value())
                    act.activation(pool_hi[:, 4 * q:4 * q + 4, :], tmp[q][:, :, :], ACT.Copy).then_inc(pool_hi_ready, 1)

                def y_split(q):
                    act.wait_ge(acc_taken[macros.slot(2)], macros.turn(2, 2))
                    macros.step()
                    act.activation(y_hi[:, 4 * q:4 * q + 4, :], tmp[q][:, :, :], ACT.Copy).then_inc(y_hi_ready, 1)

                done.step(16)
                macros.step(2)
                split(12)
                pooled_hi(0)
                split(8)
                pooled_hi(1)
                split(4)
                for q in range(2):
                    s = product(8)
                    taken(act.activation(gate_a[:, 4 * q:4 * q + 4, :], acc[s][:, :, :], ACT.Silu))
                    split(8 if q == 0 else 4)
                split(2)
                y_split(0)
                split(2)
                y_split(1)
                split(16)
                done.step(24)
                macros.step(4)

            def after_taken():
                act.wait_ge(acc_taken[macros.slot(2)], macros.turn(2, 2))
                macros.step()

            def latent(a, b):
                after_taken()
                act.activation(b[:, :, :], a[:, :, :], ACT.Square).then_inc(lat_sq, 1)
                lats.step()

            def latent_split(a, hi, k):
                act.wait_ge(lat_stat, lats.value())
                act.activation(rms_std[:, :], lat_sum, ACT.Sqrt, bias=eps[:, :], scale=1.0 / (k * P)).then_inc(lat_std, 1)
                act.wait_ge(lat_norm, lats.value())
                act.activation(hi[:, :, :], a[:, 0:k, :], ACT.Copy).then_inc(lat_hi_ready, 1)

            def swap_halves(o, x):
                for n in range(2):
                    to, x0 = n * ROPE, x[n]
                    act.activation(o[to:to + 32, :], x0[32:64, :], ACT.Copy)
                    last = act.activation(o[to + 32:to + 64, :], x0[0:32, :], ACT.Copy)
                return last

            h_split(hi=hk_hi)
            split(4)
            for m in range(2):
                square(m, kq)
            h_split()
            split(4)
            for m in range(2, 4):
                square(m, kq)
            root()
            split(1)
            done.step(8 + 1 + 8)
            latent(kq[0], kq[1])
            after_taken()
            act.activation(kr_sq[:, :], kr_raw[0:ROPE, :], ACT.Square)
            act.activation(kr_raw[ROPE:P, :], kr_raw[0:ROPE, :], ACT.Copy)
            swap_halves(kr_swap, (kr_raw, kr_raw)).then_inc(kr_ready, 1)
            split(2)
            latent_split(kq[0], c_hi, 4)
            split(6)
            act.wait_ge(lat_lo_ready, 1)
            latent(kq[0], kq[1])
            for m in range(4):
                split(8 if m < 3 else 6)
                if m == 3:
                    split_queries(2)
                done.step(8)
                after_taken()
                act.activation(gate_b[:, 4 * m:4 * m + 4, :], tmp[m % 2][:, :, :], ACT.Silu).then_inc(gate_ready, 1)
                if m == 1:
                    act.wait_ge(angle_ready, 1)
                    act.activation(sin[:, :], angle[0], ACT.Sin)
                    act.activation(cos[:, :], angle[1], ACT.Sin).then_inc(trig_ready, 1)

            def bias_store(n):
                h = slice(n * HEADS // 2, (n + 1) * HEADS // 2)
                act.dma_start(bias_lines[h, :, :], lines[h, :].unsqueeze(1).broadcast_to([HEADS // 2, P, SC])).then_inc(bias_out, 16)

            latent_split(kq[0], q_hi, 4)
            act.wait_ge(line_ready, 1)
            bias_store(0)

            pairs = Count()

            def m_stage_k(slot):
                s = product(2)
                macros.step()
                act.wait_ge(m_pv, pairs.value(1))
                act.activation(vs[slot][:, :, :], acc[s][:, 2:4, :], ACT.Copy)
                act.activation(tmp[0][:, 0:2, :], acc[s][:, 0:2, :], ACT.Square).then_inc(m_ksq, 1)

            def m_stage_q():
                s = product(2)
                macros.step()
                act.activation(tmp[0][:, 2:4, :], acc[s][:, 0:2, :], ACT.Square)
                act.activation(qr_sq[:, :], acc[s][:, 2, :], ACT.Square).then_inc(m_sq, 1)
                return s

            def m_swap(s):
                act.wait_ge(m_qk, pairs.value(1))
                swap_halves(qr_swap, (acc[s][0:ROPE, 2, :], acc[s][ROPE:P, 2, :])).then_inc(m_swapped, 1)
                pairs.step()

            def m_roots():
                act.wait_ge(m_stat, pairs.value())
                act.activation(m_root[:, :], sums[:, 1, 0:8], ACT.Sqrt, bias=eps[:, :], scale=1.0 / QK).then_inc(m_std, 1)
                act.wait_ge(m_recip, pairs.value())
                for n in range(4):
                    last = act.activation(m_diag[:, n * P:(n + 1) * P], tab("ident"), ACT.Copy, scale=m_rinv[:, n:n + 1])
                last.then_inc(m_diag_ready, 1)

            heads = Count()

            def m_turn_in():
                act.wait_ge(m_turned, heads.value())
                act.activation(m_probT[:, :, :], sums[:, :, 0:SC], ACT.Copy).then_inc(m_turned_in, 1)

            def m_spread_in():
                act.wait_ge(m_spread, pairs.value())
                act.activation(m_kinv[:, :], sums[:, 1, :], ACT.Copy, scale=QK ** -0.5).then_inc(m_kinv_ready, 1)

            outs = Count()

            def m_hi(p):
                outs.step()
                act.wait_ge(m_out_ready, outs.value())
                act.activation(h_hi[:, bass.ds(p * 2, 2), :], m_out[:, :, :], ACT.Copy).then_inc(m_mix_hi, 1)

            def m_exps():
                act.wait_ge(m_max_ready, heads.value(1))
                for half, (lo, hi) in enumerate(((0, P), (P, SC))):
                    for a in range(2):
                        last = act.activation(m_prob[:, a, lo:hi], m_prob[:, a, lo:hi], ACT.Exp, bias=m_neg[:, half, a:a + 1],
                                              accum_out=m_sum[:, half, a:a + 1])
                last.then_inc(m_exp, 1)
                heads.step()

            m_stage_k(0)
            split(2)
            m_swap(m_stage_q())
            split_queries(2)
            m_roots()
            split(2)
            m_stage_k(1)
            m_spread_in()
            q_set = m_stage_q()
            m_exps()
            m_swap(q_set)
            with loop(act, PAIRS // 2 - 1, [(slabs, 8), (done, 8), (macros, 4), (pairs, 2), (heads, 2), (outs, 2)]) as i:
                for a in range(2):
                    split_queries(2)
                    m_roots()
                    m_turn_in()
                    split(2)
                    m_stage_k(a)
                    m_spread_in()
                    m_hi(i * 2 + a)
                    q_set = m_stage_q()
                    m_exps()
                    m_swap(q_set)
            bias_store(1)
            split(2)
            m_roots()
            m_turn_in()
            m_hi(PAIRS - 2)
            m_spread_in()
            m_exps()
            split(2)
            m_turn_in()
            split(1)
            m_hi(PAIRS - 1)
            split(1)
            split(28)
            done.step(32)
            macros.step(4)

            def bias_load(n):
                act.dma_start(bias[:, :, :], bass.AP(tensor=bias_lines, offset=n * HEADS * P * SC + P - 1,
                                                     ap=[[SC - 1, P], [P * SC, HEADS], [1, TOK]])).then_inc(bias_in, 16)

            squares()
            act.wait_ge(bias_out, 32)
            bias_load(0)
            bias_store(2)
            act.dma_start(sinks[:, :], t["attn_sinks_2"][0:1, :].broadcast_to([P, HEADS])).then_inc(sinks_in, 16)
            h_split(0)
            with loop(act, 3, [(slabs, 16), (done, 16), (macros, 2)]) as i:
                for m in range(2):
                    split(8)
                    s = product(8)
                    taken(act.activation(proj[:, bass.ds(i * 8 + m * 4, 4), :], acc[s][:, :, :], ACT.Copy))
            act.activation(tmp[0][:, 0:2, :], proj[:, T_C:T_C + 2, :], ACT.Square).then_inc(lat_sq, 1)
            lats.step()
            bias_store(3)
            split(4)
            latent_split(tmp[1], lat_hi, 2)
            split(4)
            s = product(8)
            taken(act.activation(proj[:, 24:28, :], acc[s][:, :, :], ACT.Copy))
            s = product(2)
            taken(act.activation(kiwi[:, :], acc[s][0:KW, 0, :], ACT.Copy))
            split(2)

            def attention(kind):
                sm = att[kind]
                for step in range(TILES + 3):
                    if 0 <= step - 2 < TILES:
                        p = step - 2
                        act.wait_ge(sm["turned"], p + 1)
                        if p >= 2:
                            act.wait_ge(sm["pv"], p - 1)
                        act.activation(probT[p % 2][:, :, :], side[:, :, 0:SC], ACT.Copy).then_inc(sm["turned_in"], 1)
                    if step - 3 >= 0:
                        p = step - 3
                        act.wait_ge(sm["pv"], p + 1)
                        act.activation(h_hi[:, p + kind * TILES, :], sums[:, p % 2, 0:TOK], ACT.Copy).then_inc(sm["mix_hi"], 1)
                    if step < TILES:
                        pr, a = prob[step % AHEAD], step % AHEAD
                        act.wait_ge(sm["max"], step + 1)
                        for half, (lo, hi) in enumerate(((0, P), (P, SC))):
                            for e in range(2):
                                last = act.activation(pr[:, e, lo:hi], pr[:, e, lo:hi], ACT.Exp,
                                                      bias=a_neg[a][:, half, e:e + 1], accum_out=a_sum[a][:, half, e:e + 1])
                        if kind == 0:
                            last = act.activation(a_exp[a][:, :, :], a_gap[a][:, :, :], ACT.Exp)
                        last.then_inc(sm["exp"], 1)

            attention(0)
            act.wait_ge(bias_out, 64)
            bias_load(1)
            for p in range(TILES):
                act.wait_ge(idx_dots, p + 1)
                if p >= AHEAD:
                    act.wait_ge(idx_added, p - AHEAD + 1)
                act.activation(prob[p % AHEAD][:, :, :], acc_banks[p % 2][:, :, 0:SC], ACT.Relu).then_inc(idx_relu, 1)
            for o in ([kb[:, 4 * n:4 * n + 4, :] for n in range(2)], [vb_tok[:, n, :] for n in range(2)]):
                done.step(2)
                act.wait_ge(slab_used, done.value(RING))
                for n in range(2):
                    s = macros.slot(2)
                    x = acc[s][:, :, :] if len(o[n].shape) == 3 else flat(acc[s][:, :, :])
                    taken(act.activation(o[n], x, ACT.Copy))
                split(2)
            split(16)
            done.step(16)
            macros.step(4)
            attention(1)
            with loop(act, 2, [(slabs, 8), (done, 8), (macros, 2)]) as i:
                split(8)
                done.step(8)
                macros.step(2)
            squares()
            h_split(3)
            def ff_u():
                act.wait_ge(acc_taken[macros.slot(2)], macros.turn(2, 2))
                macros.step()
                act.activation(conv_silu[:, :, :], conv[:, :, :], ACT.Silu).then_inc(conv_silu_ready, 1)

            def ff_g(a):
                act.wait_ge(acc_taken[macros.slot(2)], macros.turn(2, 2))
                macros.step()
                act.activation(f_hi[a][:, :, :], f_raw[:, :, :], ACT.Copy).then_inc(f_hi_ready, 1)

            split(8)
            ff_u()
            split(8)
            ff_g(0)
            with loop(act, FBLOCKS // 2, [(slabs, 48), (macros, 12)]) as i:
                for a in range(2):
                    split(8)
                    ff_u()
                    split(8)
                    ff_g(1 - a)
                    split(8)
                    macros.step(4)
            split(8 - RING)
            macros.step(4)
            squares()
            for m in range(4):
                act.wait_ge(fin_turned, m + 1)
                if m >= 2:
                    act.wait_ge(y_stored[m % 2], 16)
                act.activation(y_tok[m % 2][:, :, :], acc_banks[m % 2], ACT.Copy).then_inc(y_copied, 1)

        @block.vector
        def _(dve):
            slabs, done, macros, norms, lats, steps = (Count() for _ in range(6))
            dve.sem_inc(lo_ready, RING)
            for s in acc_taken:
                dve.sem_inc(s, 1)
            for s in (mod_ready, m_qk):
                dve.sem_inc(s, 1)

            def link(ins):
                steps.step()
                ins.then_inc(dve_step, 1)
                dve.wait_ge(dve_step, steps.value())

            def split(n):
                for _ in range(n):
                    s = slabs.slot(RING)
                    dve.wait_ge(hi_ready, slabs.value(1))
                    dve.tensor_tensor(w_lo[s][:, :], raw[s][:, :], f32(w_hi[s][:, :]), ALU.subtract).then_inc(lo_ready, 1)
                    slabs.step()

            def split_queries(n):
                for _ in range(n):
                    s = slabs.slot(RING)
                    dve.wait_ge(hi_ready, slabs.value(1))
                    for o, x, hi in zip(query_parts(w_lo[s], True), query_parts(raw[s], False), query_parts(f32(w_hi[s]), True)):
                        last = dve.tensor_tensor(o, x, hi, ALU.subtract)
                    last.then_inc(lo_ready, 1)
                    slabs.step()

            def product(n):
                done.step(n)
                dve.wait_ge(slab_used, done.value(RING))
                return macros.slot(2)

            def taken(ins):
                ins.then_inc(acc_taken[macros.slot(2)], 1)
                macros.step()

            def col(c, n=1, rows=P):
                return vec[0:rows, c:c + n]

            link(dve.memset(ones[:, :], 1.0))
            dve.memset(eps[:, :], EPS).then_inc(const_set, 1)

            for m in range(4):
                dve.wait_ge(x_turned, m + 1)
                dve.tensor_copy(xT[:, 4 * m:4 * m + 4, :], acc[m % 2][:, :, :]).then_inc(x_ready, 1)
            split(RING)

            def norm_root():
                norms.step()
                dve.wait_ge(std_ready, norms.value())
                link(dve.reciprocal(rms_inv[:, :], rms_std[:, :]))

            def norm(gain, shift=None, inv=True, hi=h_hi, lo=h_lo):
                first = h_lows.total()

                def part(j):
                    return tmp[j // 2 % 2][:, j % 2 * 2:j % 2 * 2 + 2, :]

                def scaled(j):
                    if j >= 4:
                        dve.wait_ge(h_lo_ready, first + j - 3)
                    for n in range(2):
                        c = 2 * j + n
                        if inv:
                            last = dve.scalar_tensor_tensor(part(j)[:, n, :], xT[:, c, :], gain(c), rms_inv[:, :], ALU.mult, ALU.mult)
                        else:
                            last = dve.tensor_scalar(part(j)[:, n, :], xT[:, c, :], gain(c), None, ALU.mult)
                    last.then_inc(norm_ready, 1)

                def low(j):
                    h_lows.step()
                    dve.wait_ge(h_hi_ready, h_lows.value())
                    c = 2 * j
                    if shift is None:
                        last = dve.tensor_tensor(lo[:, c:c + 2, :], part(j), f32(hi[:, c:c + 2, :]), ALU.subtract)
                    else:
                        for n in range(2):
                            last = dve.scalar_tensor_tensor(lo[:, c + n, :], part(j)[:, n, :], mod[:, shift, c + n:c + n + 1],
                                                            f32(hi[:, c + n, :]), ALU.add, ALU.subtract)
                    last.then_inc(h_lo_ready, 1)

                scaled(0)
                scaled(1)
                for j in range(KD // 2):
                    low(j)
                    if j + 2 < KD // 2:
                        scaled(j + 2)

            h_lows = Count()
            dve.wait_ge(vec_turned, 1)
            dve.tensor_copy(vec[:, :], side[:, 0, 0:V_ROWS]).then_inc(vec_ready, 1)
            link(dve.memset(csum[:, :, 0:PAD], 0.0))
            norm_root()
            norm(lambda c: col(V_A_NORM + c))

            def add_product(n_slabs, m, scale=None):
                s = product(n_slabs)
                if scale is None:
                    taken(dve.tensor_tensor(xT[:, bass.ds(m, 4), :], acc[s][:, :, :], xT[:, bass.ds(m, 4), :], ALU.add))
                else:
                    for n in range(4):
                        x = flat(xT[:, bass.ds(m + n, 1), :])
                        last = dve.scalar_tensor_tensor(x, acc[s][:, n, :], mod[:, scale, bass.ds(m + n, 1)], x, ALU.mult, ALU.add)
                    taken(last)

            mods = Count()

            def take_mod(v):
                mods.step()
                dve.wait_ge(mod_summed, mods.value())
                m = flat(mod[:, bass.ds(v, 1), :])
                dve.tensor_tensor(m, side[:, 1, 0:KD], vec[:, bass.ds(v * KD + V_BMOD, KD)], ALU.add).then_inc(mod_ready, 1)

            dve.wait_ge(table_in, 16)
            pools, ys = Count(), Count()
            with loop(dve, GROUPS, [(slabs, 56), (done, 56), (macros, 10), (pools, 2), (ys, 2), (steps, 6), (mods, 1)]) as g:
                window = (g * g * g + g * 5) // 3 + 2

                def pool(q):
                    s = product(8)
                    for n in range(4):
                        last = dve.tensor_tensor_scan(csum[:, n, PAD:PAD + TOK], ones[:, :], acc[s][:, n, :], 0.0, ALU.mult, ALU.add)
                    link(last)
                    link(dve.tensor_tensor(tmp[q][:, :, :], csum[:, :, PAD:PAD + TOK],
                                           csum[:, :, bass.ds(PAD - window, TOK)], ALU.subtract))
                    rc0 = cols["rcount"][0]
                    rcount = table[:, bass.ds(g * PAD + rc0, PAD)].unsqueeze(1).broadcast_to([P, 4, PAD])
                    link(dve.tensor_tensor(first16[:, :, :], tmp[q][:, :, 0:PAD], rcount, ALU.mult))
                    dve.tensor_tensor(first16[:, :, :], first16[:, :, :], acc[s][:, :, 0:PAD], ALU.subtract)
                    dve.scalar_tensor_tensor(tmp[q][:, :, :], tmp[q][:, :, :], table[:, bass.ds(g + cols["rwindow"][0], 1)],
                                             acc[s][:, :, :], ALU.mult, ALU.subtract).then_inc(acc_taken[s], 1)
                    dve.wait_ge(acc_taken[s], macros.turn(2, 2))
                    macros.step()
                    dve.tensor_copy(tmp[q][:, :, 0:PAD], first16[:, :, :]).then_inc(pool_ready, 1)

                def pooled_lo(q):
                    pools.step()
                    dve.wait_ge(pool_hi_ready, pools.value())
                    c = slice(4 * q, 4 * q + 4)
                    dve.tensor_tensor(pool_lo[:, c, :], tmp[q][:, :, :], f32(pool_hi[:, c, :]), ALU.subtract).then_inc(pool_lo_ready, 1)

                def gate(q):
                    s = product(4)
                    for n in range(4):
                        last = dve.scalar_tensor_tensor(tmp[q][:, n, :], acc[s][:, n, :], vec[:, bass.ds(g * 8 + (V_A_SCALE + 4 * q + n), 1)],
                                                        gate_a[:, 4 * q + n, :], ALU.mult, ALU.mult)
                    taken(last)

                def y_low(q):
                    ys.step()
                    dve.wait_ge(y_hi_ready, ys.value())
                    c = slice(4 * q, 4 * q + 4)
                    dve.tensor_tensor(y_lo[:, c, :], tmp[q][:, :, :], f32(y_hi[:, c, :]), ALU.subtract).then_inc(y_lo_ready, 1)

                split(8)
                pool(0)
                split(4)
                pooled_lo(0)
                split(4)
                pool(1)
                split(4)
                pooled_lo(1)
                split(4 + 8 + 4)
                for q in range(2):
                    done.step(8)
                    dve.wait_ge(acc_taken[macros.slot(2)], macros.turn(2, 2))
                    macros.step()
                gate(0)
                split(2)
                y_low(0)
                split(2)
                gate(1)
                y_low(1)
                split(4)
                for m in range(4):
                    add_product(4, 4 * m)
                    if m < 3:
                        split(4)
                take_mod(g)

            norm(lambda c: col(V_KV_NORM + c), inv=False, hi=hk_hi, lo=hk_lo)
            split(4)
            norm(lambda c: col(V_B_NORM + c), inv=False)
            split(4)
            norm_root()
            inv4 = rms_inv[:, :].unsqueeze(1).broadcast_to([P, 4, TOK])

            def latent(a, k, gain, hi, lo, src=None):
                lats.step()
                dve.wait_ge(lat_std, lats.value())
                link(dve.reciprocal(lat_inv[:, :], rms_std[:, :]))
                for n in range(k):
                    last = dve.scalar_tensor_tensor(a[:, n, :], (src or (lambda n: a[:, n, :]))(n), col(gain + n),
                                                    lat_inv[:, :], ALU.mult, ALU.mult)
                last.then_inc(lat_norm, 1)
                dve.wait_ge(lat_hi_ready, lats.value())
                dve.tensor_tensor(lo[:, :, :], a[:, 0:k, :], f32(hi[:, :, :]), ALU.subtract).then_inc(lat_lo_ready, 1)

            s = product(8)
            taken(dve.tensor_tensor(kq[0][:, :, :], acc[s][:, :, :], inv4, ALU.mult))
            split(1)
            s = product(1)
            taken(dve.tensor_tensor(kr_raw[0:ROPE, :], acc[s][0:ROPE, 0, :], rms_inv[0:ROPE, :], ALU.mult))
            split(2)
            latent(kq[0], 4, V_KV_LAT, c_hi, c_lo)
            split(6)
            dve.wait_ge(lat_lo_ready, 1)
            s = product(8)
            taken(dve.tensor_tensor(kq[0][:, :, :], acc[s][:, :, :], inv4, ALU.mult))

            def rope_angles():
                dve.wait_ge(pos_in, 16)
                link(dve.tensor_copy(angle[2], pos[:, :]))
                link(dve.tensor_scalar(angle[2], angle[2], tab("inv_freq"), None, ALU.mult))
                for n, quarter in ((0, 0.0), (1, 0.25)):
                    link(dve.tensor_scalar(angle[3], angle[2], float(1 / (2 * np.pi)), quarter, ALU.mult, ALU.add))
                    link(dve.tensor_scalar(angle[3], angle[3], ROUND, None, ALU.add))
                    link(dve.tensor_scalar(angle[3], angle[3], -ROUND, None, ALU.add))
                    link(dve.scalar_tensor_tensor(angle[n], angle[3], -TWO_PI_A, angle[2], ALU.mult, ALU.add))
                    link(dve.scalar_tensor_tensor(angle[n], angle[3], -TWO_PI_B, angle[n], ALU.mult, ALU.add))
                    link(dve.scalar_tensor_tensor(angle[n], angle[3], -TWO_PI_C, angle[n], ALU.mult, ALU.add))
                    link(dve.tensor_scalar(angle[n], angle[n], quarter * float(2 * np.pi), None, ALU.add))
                    last = dve.tensor_scalar(angle[n], angle[n], PI_CLAMP, -PI_CLAMP, ALU.min, ALU.max)
                    if n == 0:
                        link(last)
                last.then_inc(angle_ready, 1)

            def rope_keys():
                dve.wait_ge(trig_ready, 1)
                link(dve.tensor_scalar(sin[:, :], sin[:, :], tab("rope_sign"), None, ALU.mult))
                dve.wait_ge(kr_ready, 1)
                dve.scalar_tensor_tensor(kr_rot[:, :], kr_raw[:, :], col(V_KR), cos[:, :], ALU.mult, ALU.mult)
                link(dve.scalar_tensor_tensor(kr_swap[:, :], kr_swap[:, :], col(V_KRS), sin[:, :], ALU.mult, ALU.mult))
                dve.tensor_tensor(kr_rot[:, :], kr_rot[:, :], kr_swap[:, :], ALU.add).then_inc(kr_done, 1)

            dve.wait_ge(line_sum, 1)
            dve.tensor_copy(lines[:, :], side[0:2 * HEADS, 1, 0:SC]).then_inc(line_ready, 1)
            for m in range(4):
                split(8 if m < 3 else 6)
                if m == 3:
                    split_queries(2)
                if m == 1:
                    rope_angles()
                if m == 2:
                    rope_keys()
                s = product(8)
                if m >= 2:
                    dve.wait_ge(gate_ready, m - 1)
                taken(dve.tensor_tensor(tmp[m % 2][:, :, :], acc[s][:, :, :], inv4, ALU.mult))
            latent(kq[0], 4, V_Q_LAT, q_hi, q_lo)
            take_mod(4)

            pairs, heads = Count(), Count()

            def m_take_q(slot):
                pairs.step()
                dve.wait_ge(m_swapped, pairs.value())
                s = product(2)
                dve.tensor_scalar(kq[slot][:, 2:4, :], acc[s][:, 0:2, :], col(V_QN), None, ALU.mult)
                taken(dve.scalar_tensor_tensor(qr[slot][:, :], acc[s][:, 2, :], col(V_QR), cos[:, :], ALU.mult, ALU.mult))
                link(dve.scalar_tensor_tensor(qr_swap[:, :], qr_swap[:, :], col(V_QRS), sin[:, :], ALU.mult, ALU.mult))
                dve.tensor_tensor(qr[slot][:, :], qr[slot][:, :], qr_swap[:, :], ALU.add).then_inc(m_qk, 1)

            def m_take_k(slot):
                dve.wait_ge(m_ksq, pairs.value(1))
                s = product(2)
                taken(dve.tensor_scalar(kq[slot][:, 0:2, :], acc[s][:, 0:2, :], col(V_KN), None, ALU.mult))
                sq = tmp[0][0:ROPE, 0:2, :]
                dve.tensor_tensor(sq, sq, kr_sq[:, :].unsqueeze(1).broadcast_to([ROPE, 2, TOK]), ALU.add).then_inc(m_folded, 1)

            def m_reciprocals():
                dve.wait_ge(m_std, pairs.value())
                dve.reciprocal(m_rinv[:, :], m_root[:, :]).then_inc(m_recip, 1)

            def row_max(mx, pr):
                dve.tensor_reduce(mx[:, 0, :], pr[:, :, 0:P], AX.X, ALU.max)
                link(dve.tensor_reduce(mx[:, 1, :], pr[:, :, P:SC], AX.X, ALU.max))

            def scale_rows(pr, inv):
                dve.tensor_tensor(pr[:, :, 0:P], pr[:, :, 0:P], inv[:, 0, :].unsqueeze(2).broadcast_to([P, 2, P]), ALU.mult)
                return dve.tensor_tensor(pr[:, :, P:SC], pr[:, :, P:SC], inv[:, 1, :].unsqueeze(2).broadcast_to([P, 2, TOK]), ALU.mult)

            def m_soft():
                heads.step()
                dve.wait_ge(m_score, heads.value())
                dve.wait_ge(m_kinv_ready, heads.value())
                for e in range(2):
                    for half, (lo, n) in enumerate(((0, P), (P, TOK))):
                        last = dve.scalar_tensor_tensor(m_prob[:, e, lo:lo + n], side[:, e, lo:lo + n], m_rinv[:, 4 + 2 * e + half:5 + 2 * e + half],
                                                        m_kinv[:, e * TOK:e * TOK + n], ALU.mult, ALU.mult)
                link(last)
                link(dve.tensor_tensor(m_prob[:, :, :], m_prob[:, :, :], tab("chunk_mask").unsqueeze(1).broadcast_to([P, 2, SC]), ALU.add))
                row_max(m_max, m_prob)
                dve.tensor_scalar(m_neg[:, :, :], m_max[:, :, :], -1.0, None, ALU.mult).then_inc(m_max_ready, 1)

            def m_scale():
                dve.wait_ge(m_exp, heads.value())
                link(dve.reciprocal(m_inv[:, :, :], m_sum[:, :, :]))
                scale_rows(m_prob, m_inv).then_inc(m_prob_ready, 1)

            outs = Count()

            def m_gate(p):
                outs.step()
                dve.wait_ge(m_pv, outs.value(2))
                dve.tensor_tensor(flat(m_out[:, :, :]), sums[:, 0, :], flat(gate_b[:, bass.ds(p * 2, 2), :]), ALU.mult)\
                    .then_inc(m_out_ready, 1)

            def m_low(p):
                dve.wait_ge(m_mix_hi, outs.value())
                dve.tensor_tensor(h_lo[:, bass.ds(p * 2, 2), :], m_out[:, :, :], f32(h_hi[:, bass.ds(p * 2, 2), :]), ALU.subtract)\
                    .then_inc(mix_lo, 1)

            m_take_k(0)
            split(2)
            m_take_q(0)
            split_queries(2)
            m_reciprocals()
            split(2)
            m_take_k(1)
            m_soft()
            m_scale()
            with loop(dve, PAIRS // 2 - 1, [(slabs, 8), (done, 8), (macros, 4), (pairs, 2), (heads, 2), (outs, 2), (steps, 10)]) as i:
                for a in range(2):
                    m_take_q(1 - a)
                    split_queries(2)
                    m_reciprocals()
                    split(2)
                    m_take_k(a)
                    m_gate(i * 2 + a)
                    m_soft()
                    m_scale()
                    m_low(i * 2 + a)
            m_take_q(1)
            split(2)
            m_reciprocals()
            m_gate(PAIRS - 2)
            m_low(PAIRS - 2)
            m_soft()
            m_scale()
            split(3)
            dve.wait_ge(mix_lo, PAIRS - 1)
            m_gate(PAIRS - 1)
            m_low(PAIRS - 1)
            split(1 + 4)
            add_product(8, 0)
            for m in range(1, 4):
                split(8)
                add_product(8, 4 * m)

            dve.wait_ge(mod_ready, 6)
            dve.scalar_tensor_tensor(gain2[:, :], mod[:, 4, :], 1.0, col(V_NORM_FFN, KD), ALU.add, ALU.mult)
            link(dve.scalar_tensor_tensor(gain1[:, :], mod[:, 1, :], 1.0, col(V_NORM_ATTN, KD), ALU.add, ALU.mult))
            norm_root()
            norm(lambda c: gain1[:, c:c + 1], shift=0)
            take_mod(5)
            with loop(dve, 3, [(slabs, 16), (done, 16), (macros, 2)]) as i:
                split(16)
                done.step(16)
                macros.step(2)
            split(4)
            latent(tmp[1], 2, V_KV_NORM2, lat_hi, lat_lo, src=lambda n: proj[:, T_C + n, :])
            split(4)
            dve.wait_ge(side_done, 1)
            dve.tensor_copy(flat(ka_dup[:, :, :]), side[:, 0, :])
            dve.tensor_copy(flat(va_tok[:, :, :]), side[:, 1, 0:TOK]).then_inc(side_taken, 1)
            split(2)
            done.step(8 + 2)
            macros.step(2)
            dve.wait_ge(side_done, 2)
            dve.tensor_copy(ki_dup[:, :], side[:, 1, 0:TOK])
            wi = sums[:, 0, 0:2 * P].rearrange("p (h n) -> p h n", h=2)
            dve.tensor_scalar(wi_tok[:, :, :], wi[:, :, HD:KW], IDX_SCALE, None, ALU.mult).then_inc(side_taken, 1)
            dve.wait_ge(sinks_in, 16)

            def attention(kind):
                sm = att[kind]

                def softmax(p):
                    dve.wait_ge(sm["score"], p + 1)
                    if p >= AHEAD:
                        dve.wait_ge(sm["turned"], p - AHEAD + 1)
                    a, sc = p % AHEAD, acc_banks[p % 2]
                    pr, heads = prob[a], slice(2 * p, 2 * p + 2)
                    dve.scalar_tensor_tensor(pr[:, :, 0:P], sc[:, :, 0:P], HD ** -0.5, bias[:, heads, P:TOK], ALU.mult, ALU.add)
                    link(dve.scalar_tensor_tensor(pr[:, :, P:SC], sc[:, :, P:SC], HD ** -0.5, bias[:, heads, :], ALU.mult, ALU.add))
                    if kind == 1:
                        link(dve.tensor_tensor(pr[:, :, :], pr[:, :, :], sel[:, :].unsqueeze(1).broadcast_to([P, 2, SC]), ALU.add))
                    row_max(a_max[a], pr)
                    if kind == 0:
                        sink = sinks[:, heads].unsqueeze(1).broadcast_to([P, 2, 2])
                        link(dve.tensor_tensor(a_max[a][:, :, :], a_max[a][:, :, :], sink, ALU.max))
                        dve.tensor_tensor(a_gap[a][:, :, :], sink, a_max[a][:, :, :], ALU.subtract)
                    dve.tensor_scalar(a_neg[a][:, :, :], a_max[a][:, :, :], -1.0, None, ALU.mult).then_inc(sm["max"], 1)

                def reciprocals(p):
                    a = p % AHEAD
                    dve.wait_ge(sm["exp"], p + 1)
                    if kind == 0:
                        link(dve.tensor_tensor(a_sum[a][:, :, :], a_sum[a][:, :, :], a_exp[a][:, :, :], ALU.add))
                    dve.reciprocal(a_inv[a][:, :, :], a_sum[a][:, :, :]).then_inc(sm["inv"], 1)

                def mix_low(p):
                    dve.wait_ge(sm["mix_hi"], p + 1)
                    c = p + kind * TILES
                    dve.tensor_tensor(h_lo[:, c, :], sums[:, p % 2, 0:TOK], f32(h_hi[:, c, :]), ALU.subtract).then_inc(sm["mix_lo"], 1)

                dve.wait_ge(bias_ready, kind + 1)
                for step in range(TILES + 3):
                    if step < TILES:
                        softmax(step)
                    if 0 <= step - 1 < TILES:
                        reciprocals(step - 1)
                    if step - 3 >= 0:
                        mix_low(step - 3)

            attention(0)

            dve.tensor_copy(idx[:, 0:P], tab("causal_mask", P, TOK))
            link(dve.tensor_copy(idx[:, P:SC], tab("causal_mask")))
            halves = ((0, slice(0, P)), (1, slice(P, SC)))
            for p in range(TILES):
                dve.wait_ge(idx_relu, p + 1)
                for e in range(2):
                    for half, c in halves:
                        w = wi_tok[:, half, 2 * p + e:2 * p + e + 1]
                        last = dve.scalar_tensor_tensor(idx[:, c], prob[p % AHEAD][:, e, c], w, idx[:, c], ALU.mult, ALU.add)
                    if e == 0:
                        link(last)
                last.then_inc(idx_added, 1)
                dve.wait_ge(idx_added, p + 1)
            done.step(4)
            macros.step(4)
            link(dve.tensor_copy(idx_work[:, :], idx[:, :]))
            for r in range(TOPK // 8):
                for half, c in halves:
                    last = dve.max(top8[:, half, :], idx_work[:, c])
                link(last)
                if r < TOPK // 8 - 1:
                    for half, c in halves:
                        last = dve.match_replace(idx_work[:, c], top8[:, half, :], idx_work[:, c], -3e38)
                    link(last)
                split(1)
            add_product(4, 0, scale=2)
            cum, equal = prob[0][:, 0, :], prob[0][:, 1, :]
            for half, c in halves:
                thr = top8[:, half, 7:8]
                dve.tensor_scalar(idx_work[:, c], idx[:, c], thr, None, ALU.is_gt)
                last = dve.tensor_scalar(equal[:, c], idx[:, c], thr, None, ALU.is_equal)
            link(last)
            for half, c in halves:
                dve.tensor_reduce(quota[:, half:half + 1], idx_work[:, c], AX.X, ALU.add)
                last = dve.tensor_tensor_scan(cum[:, c], ones[:, 0:c.stop - c.start], equal[:, c], 0.0, ALU.mult, ALU.add)
            link(last)
            link(dve.tensor_scalar(quota[:, :], quota[:, :], -1.0, float(TOPK), ALU.mult, ALU.add))
            for half, c in halves:
                last = dve.scalar_tensor_tensor(sel[:, c], cum[:, c], quota[:, half:half + 1], equal[:, c], ALU.is_le, ALU.mult)
            link(last)
            link(dve.tensor_tensor(sel[:, :], sel[:, :], idx_work[:, :], ALU.add))
            link(dve.tensor_scalar(sel[:, :], sel[:, :], -1.0, -NEG, ALU.add, ALU.mult))
            for m in range(1, 4):
                split(4)
                add_product(4, 4 * m, scale=2)
            attention(1)

            with loop(dve, 2, [(slabs, 8), (done, 8), (macros, 2)]) as i:
                for m in range(2):
                    split(4)
                    add_product(4, i * 8 + 4 * m, scale=2)
            norm_root()
            norm(lambda c: gain2[:, c:c + 1], shift=3)

            ffs = Count()

            def ff_conv(i):
                ffs.step()
                s = product(8)

                def tap(w, n):
                    return vec[:, bass.ds(i * 4 + (V_CONV + w * KF + n), 1)]

                for n in range(4):
                    last = dve.tensor_scalar(conv[:, n, :], acc[s][:, n, :], tap(2, n), vec[:, bass.ds(i * 4 + (V_CONVB + n), 1)], ALU.mult, ALU.add)
                link(last)
                for n in range(4):
                    last = dve.scalar_tensor_tensor(conv[:, n, 1:TOK], acc[s][:, n, 0:TOK - 1], tap(1, n), conv[:, n, 1:TOK], ALU.mult, ALU.add)
                link(last)
                for n in range(4):
                    last = dve.scalar_tensor_tensor(conv[:, n, 2:TOK], acc[s][:, n, 0:TOK - 2], tap(0, n), conv[:, n, 2:TOK], ALU.mult, ALU.add)
                taken(last)

            def ff_gate(a):
                s = product(8)
                dve.wait_ge(conv_silu_ready, ffs.value())
                taken(dve.tensor_tensor(f_raw[:, :, :], acc[s][:, :, :], conv_silu[:, :, :], ALU.mult))

            def ff_low(a):
                dve.wait_ge(f_hi_ready, ffs.value())
                dve.tensor_tensor(f_lo[a][:, :, :], f_raw[:, :, :], f32(f_hi[a][:, :, :]), ALU.subtract).then_inc(f_lo_ready, 1)

            split(8)
            ff_conv(0)
            split(8)
            ff_gate(0)
            ff_low(0)
            with loop(dve, FBLOCKS // 2, [(slabs, 48), (done, 48), (macros, 12), (ffs, 2), (steps, 4)]) as i:
                for a in range(2):
                    split(8)
                    ff_conv(i * 2 + (a + 1))
                    split(8)
                    ff_gate(1 - a)
                    ff_low(1 - a)
                    for m in range(4):
                        split(2)
                        add_product(2, 4 * m, scale=5)
            for m in range(4):
                if m < 2:
                    split(2)
                add_product(2, 4 * m, scale=5)

            norm_root()
            for m in range(4):
                if m >= 2:
                    dve.wait_ge(fin_turned, m - 1)
                for n in range(4):
                    last = dve.scalar_tensor_tensor(tmp[m % 2][:, n, :], xT[:, 4 * m + n, :], col(V_NORM_FIN + 4 * m + n),
                                                    rms_inv[:, :], ALU.mult, ALU.mult)
                last.then_inc(fin_ready, 1)

        @block.tensor
        def _(pe):
            slabs, macros, groups, h_groups, lats = (Count() for _ in range(5))
            pe.sem_inc(slab_used, RING)
            pe.sem_inc(m_pv, 2)
            ident = tab("ident")

            def mm(o, lhsT, rhs, start=False, stop=False):
                return pe.matmul(o, lhsT, rhs, start=start, stop=stop, skip_group_check=True)

            def w_slot(k, n):
                s = slabs.slot(RING)
                hi = w_hi[s][:, 0:k * n].rearrange("p (k n) -> p k n", k=k)
                lo = w_lo[s][:, 0:k * n].rearrange("p (k n) -> p k n", k=k)
                pe.wait_ge(lo_ready, slabs.value(RING + 1))
                return hi, lo

            def set_free():
                s = macros.slot(2)
                pe.wait_ge(acc_taken[s], macros.turn(2, 1))
                macros.step()
                return s

            def gemm(n_slabs, x_hi, x_lo, tiles, k=SLAB_K, n=SLAB_N, before=None, x0=0):
                a = acc[set_free()]
                for s in range(n_slabs):
                    hi, lo = w_slot(k, n)
                    if before:
                        before(s)
                    for i, (c0, rows) in enumerate(tiles):
                        o = a[0:rows, i, :]
                        for kk in range(k):
                            x = s * k + kk + x0
                            first = s == 0 and kk == 0 and i % 2 == 0
                            end = s == n_slabs - 1 and kk == k - 1 and (i % 2 == 1 or i == len(tiles) - 1)
                            mm(o, hi[:, kk, c0:c0 + rows], x_hi[:, x, :], start=first)
                            mm(o, hi[:, kk, c0:c0 + rows], x_lo[:, x, :])
                            last = mm(o, lo[:, kk, c0:c0 + rows], x_hi[:, x, :], stop=end)
                    last.then_inc(slab_used, 1)
                    slabs.step()

            four = [(i * P, P) for i in range(4)]

            def sum_squares(k_tiles, o, x, first, end):
                for n in range(k_tiles):
                    last = mm(o, ones[:, 0:P], x[:, n, :], start=first and n == 0, stop=end and n == k_tiles - 1)
                return last

            def norm_sums(buffers=tmp):
                for m in range(4):
                    groups.step()
                    pe.wait_ge(sq_ready, groups.value())
                    sum_squares(4, rms_sum, buffers[m % 2], m == 0, m == 3).then_inc(sq_summed, 1)

            def h_ready(base):
                def before(s):
                    pe.wait_ge(h_lo_ready, base + s + 1)
                return before

            pe.wait_ge(ident_in, 16)
            pe.wait_ge(x_in, 16)
            for m in range(4):
                if m >= 2:
                    pe.wait_ge(x_ready, m - 1)
                for n in range(4):
                    for half in range(HALVES):
                        c = (4 * m + n) * P
                        last = pe.transpose(acc[m % 2][:, n, half * P:(half + 1) * P], x_tok[:, half, c:c + P], ident)
                last.then_inc(x_turned, 1)
            pe.wait_ge(const_set, 1)
            norm_sums()
            pe.wait_ge(vec_in, 16 * N_VEC)
            for r, n in enumerate((P, P, P, V_ROWS - 3 * P)):
                last = pe.transpose(side[:, 0, r * P:r * P + n], rows[r][0:n, :], ident[0:n, 0:n])
            last.then_inc(vec_turned, 1)

            mods = Count()

            def mod_sum():
                mods.step()
                pe.wait_ge(mod_step, mods.value() * (4 * KD - 2))
                for n in range(KD):
                    last = mm(side[:, 1, n:n + 1], mod_acc[:, n * P:(n + 1) * P], ones[:, 0:1], start=n == 0, stop=n == KD - 1)
                last.then_inc(mod_summed, 1)

            pools, ys = Count(), Count()
            with loop(pe, GROUPS, [(slabs, 56), (macros, 10), (pools, 2), (ys, 2), (mods, 1)]) as g:
                for m in range(4):
                    gemm(8, h_hi, h_lo, four, before=h_ready(0))

                def pooled(s):
                    if s % 2 == 0:
                        pe.wait_ge(pool_lo_ready, pools.value(s // 2 + 1))

                def gated(s):
                    if s % 2 == 0:
                        pe.wait_ge(y_lo_ready, ys.value(s // 2 + 1))

                for m in range(2):
                    gemm(4, pool_hi, pool_lo, four, before=pooled)
                pools.step(2)
                for m in range(4):
                    gemm(4, y_hi, y_lo, four, before=gated)
                ys.step(2)
                mod_sum()

            gemm(8, hk_hi, hk_lo, four, before=h_ready(8))
            norm_sums(kq)
            gemm(1, hk_hi, hk_lo, [(0, ROPE)], k=KD, n=ROPE)

            def latent_sum(x, k):
                lats.step()
                pe.wait_ge(lat_sq, lats.value())
                sum_squares(k, lat_sum, x, True, True).then_inc(lat_stat, 1)

            def query_latent(s):
                h_ready(16)(s)
                if s == 3:
                    latent_sum(kq[1], 4)

            gemm(8, h_hi, h_lo, four, before=query_latent)
            pe.wait_ge(rel_in, 16)
            pe.wait_ge(table_in, 16)
            pe.wait_ge(mod_ready, 5)
            mm(side[0:2 * HEADS, 1, 0:SC], rel[:, :], tab("onehot", rows=BUCKETS), start=True, stop=True).then_inc(line_sum, 1)
            with loop(pe, 2, [(slabs, 16), (macros, 2)]) as i:
                for m in range(2):
                    gemm(8, h_hi, h_lo, four)
            latent_sum(kq[1], 4)
            pe.wait_ge(line_ready, 1)
            mod_sum()

            pairs, heads = Count(), Count()
            pe.wait_ge(lat_lo_ready, 1)
            pe.wait_ge(kr_done, 1)
            pe.wait_ge(mod_ready, 6)

            def m_keys(between=None):
                a = acc[set_free()]
                for s in range(2):
                    hi, lo = w_slot(2, 512)
                    for e in range(2):
                        for kk in range(2):
                            x = 2 * s + kk
                            c = slice(e * (NOPE + VD), e * (NOPE + VD) + NOPE)
                            mm(a[:, e, :], hi[:, kk, c], c_hi[:, x, :], start=s == 0 and kk == 0 and e == 0)
                            mm(a[:, e, :], hi[:, kk, c], c_lo[:, x, :])
                            mm(a[:, e, :], lo[:, kk, c], c_hi[:, x, :], stop=s == 1 and kk == 1 and e == 1)
                    for half in range(HALVES):
                        o = a[:, 2 + half, :].rearrange("p (e d) -> p e d", e=2)
                        tok = slice(half * P, (half + 1) * P)
                        for kk in range(2):
                            x = 2 * s + kk
                            v_hi = hi[:, kk, :].rearrange("p (e d) -> p e d", e=2)[:, :, NOPE:NOPE + VD]
                            v_lo = lo[:, kk, :].rearrange("p (e d) -> p e d", e=2)[:, :, NOPE:NOPE + VD]
                            mm(o, c_hi[:, x, tok], v_hi, start=s == 0 and kk == 0 and half == 0)
                            mm(o, c_hi[:, x, tok], v_lo)
                            last = mm(o, c_lo[:, x, tok], v_hi, stop=s == 1 and kk == 1 and half == 1)
                    last.then_inc(slab_used, 1)
                    slabs.step()
                    if s == 0 and between:
                        between()

            def m_queries(before=None):
                gemm(2, q_hi, q_lo, four[0:3], n=2 * QK, before=before)

            def m_sums(first=False):
                pairs.step()
                pe.wait_ge(m_folded, pairs.value())
                pe.wait_ge(m_sq, pairs.value())
                if not first:
                    pe.wait_ge(m_kinv_ready, heads.value())
                for e in range(4):
                    for half in range(HALVES):
                        tok = slice(half * P, (half + 1) * P)
                        o = sums[:, 1, 2 * e + half:2 * e + half + 1]
                        mm(o, tmp[0][:, e, tok], ones[:, 0:1], start=e == 0 and half == 0)
                for half in range(HALVES):
                    last = mm(sums[:, 1, 4 + half:8:2], qr_sq[:, half * P:(half + 1) * P], tab("head_rows"), stop=half == 1)
                last.then_inc(m_stat, 1)

            def turn(o, pr):
                for e in range(2):
                    for b in range(3):
                        c = slice(b * P, (b + 1) * P)
                        last = pe.transpose(o[:, e, c], pr[:, e, c], ident)
                return last

            def weigh(o, v0, v1, pT, start, stop):
                mm(o[:, 0:P], v0, pT[:, 0:P], start=start)
                mm(o[:, P:TOK], v0, pT[:, P:2 * P])
                return mm(o[:, P:TOK], v1, pT[:, 2 * P:SC], stop=stop)

            def m_turn():
                pe.wait_ge(m_prob_ready, heads.value())
                turn(sums, m_prob).then_inc(m_turned, 1)

            def m_output(slot):
                pe.wait_ge(m_turned_in, heads.value())
                for e in range(2):
                    d = slice(e * VD, (e + 1) * VD)
                    last = weigh(sums[:, 0, e * TOK:(e + 1) * TOK], vs[slot][:, 0, d], vs[slot][:, 1, d], m_probT[:, e, :], e == 0, e == 1)
                last.then_inc(m_pv, 1)

            def m_scores(slot):
                pe.wait_ge(m_qk, pairs.value(1))
                for e in range(2):
                    for half, (lo, n) in enumerate(((0, P), (P, TOK))):
                        tok = slice(half * P, (half + 1) * P)
                        o = side[:, e, lo:lo + n]
                        mm(o, kq[slot][:, 2 + e, tok], kq[slot][:, e, 0:n], start=half == 0)
                        r = slice(e * ROPE, (e + 1) * ROPE)
                        last = mm(o, qr[slot][r, tok], kr_rot[r, 0:n], stop=half == 1)
                last.then_inc(m_score, 1)

            def m_spreads(s):
                if s == 0:
                    return
                pe.wait_ge(m_diag_ready, pairs.value())
                mm(sums[:, 1, :], ones[:, 0:P], m_diag[:, :], start=True, stop=True).then_inc(m_spread, 1)
                heads.step()

            m_keys()
            pe.wait_ge(lat_lo_ready, 2)
            m_queries()
            m_keys(lambda: m_sums(first=True))
            m_scores(0)
            m_queries(m_spreads)
            with loop(pe, PAIRS // 2 - 1, [(slabs, 8), (macros, 4), (pairs, 2), (heads, 2)]) as i:
                for a in range(2):
                    m_keys(m_sums)
                    pe.wait_ge(m_std, pairs.value())
                    m_turn()
                    m_scores(1 - a)
                    m_output(a)
                    m_queries(m_spreads)
            m_sums()
            pe.wait_ge(m_std, pairs.value())
            m_turn()
            m_scores(1)
            m_output(0)
            m_spreads(1)

            def last_pair(s):
                if s == 0:
                    pe.wait_ge(mix_lo, PAIRS - 1)
                if s == 4:
                    m_turn()
                if s == 5:
                    m_output(1)
                if s == 7:
                    pe.wait_ge(mix_lo, PAIRS)

            gemm(8, h_hi, h_lo, four, before=last_pair)
            for m in range(1, 4):
                gemm(8, h_hi, h_lo, four)

            norm_sums()
            mod_sum()
            with loop(pe, 3, [(slabs, 16), (macros, 2)]) as i:
                for m in range(2):
                    gemm(8, h_hi, h_lo, four, before=h_ready(24))
            gemm(8, h_hi, h_lo, four, before=lambda s: s == 2 and latent_sum(tmp[0], 2))
            by = macros.total() - 2
            pe.wait_ge(acc_taken[by % 2], by // 2 + 2)
            pe.wait_ge(mod_ready, 7)
            for n in range(2):
                mm(side[:, 0, n * TOK:(n + 1) * TOK], tab(f"dup{n}"), proj[:, T_KA, :], start=n == 0, stop=n == 1)
            for half in range(HALVES):
                tok = slice(half * P, (half + 1) * P)
                last = pe.transpose(side[:, 1, tok], proj[:, T_VA, tok], ident)
            last.then_inc(side_done, 1)
            gemm(2, h_hi, h_lo, [(0, KW)], k=8, n=KW)
            pe.wait_ge(acc_taken[(macros.total() - 1) % 2], (macros.total() - 1) // 2 + 2)
            pe.wait_ge(side_taken, 1)
            mm(side[:, 1, 0:TOK], tab("dup0", rows=HD), kiwi[0:HD, :], start=True, stop=True)
            pe.wait_ge(std_ready, 3)
            for half in range(HALVES):
                tok = slice(half * P, (half + 1) * P)
                last = pe.transpose(sums[:, 0, half * P:half * P + KW], kiwi[:, tok], ident[0:KW, 0:KW])
            last.then_inc(side_done, 1)
            for s in range(2):
                pe.wait_ge(acc_taken[s], (macros.total() + 1 - s) // 2 + 1)
            pe.wait_ge(side_taken, 2)

            def tile_scores(o, q, k):
                for e in range(2):
                    d = slice(e * HD, (e + 1) * HD)
                    mm(o[:, e, 0:P], q[d, 0:P], k[d, 0:P], start=True)
                    last = mm(o[:, e, P:SC], q[d, P:TOK], k[d, :], stop=True)
                return last

            def attention(kind):
                sm = att[kind]

                def scores(p):
                    if p >= 2:
                        pe.wait_ge(sm["max"], p - 1)
                    q, k = (proj[:, p, :], ka_dup[:, p // 4, :]) if kind == 0 else (proj[:, T_QB + p, :], kb[:, p, :])
                    tile_scores(acc_banks[p % 2], q, k).then_inc(sm["score"], 1)

                def turned(p):
                    pe.wait_ge(sm["prob"], p + 1)
                    if p >= 1:
                        pe.wait_ge(sm["turned_in"], p)
                    turn(side, prob[p % AHEAD]).then_inc(sm["turned"], 1)

                def output(p):
                    pe.wait_ge(sm["turned_in"], p + 1)
                    if p >= 2:
                        pe.wait_ge(sm["mix_lo"], p - 1)
                    for e in range(2):
                        if kind == 0:
                            v0, v1 = (va_tok[:, half, p // 4 * HD:(p // 4 + 1) * HD] for half in range(HALVES))
                        else:
                            v0, v1 = (vb_tok[:, half, (2 * p + e) * HD:(2 * p + e + 1) * HD] for half in range(HALVES))
                        last = weigh(sums[e * HD:(e + 1) * HD, p % 2, 0:TOK], v0, v1, probT[p % 2][:, e, :], True, True)
                    last.then_inc(sm["pv"], 1)

                scores(0)
                for step in range(TILES + 2):
                    if step >= 2:
                        turned(step - 2)
                    if step + 1 < TILES:
                        scores(step + 1)
                    if step >= 2:
                        output(step - 2)

            attention(0)
            for p in range(TILES):
                if p >= 2:
                    pe.wait_ge(idx_relu, p - 1)
                tile_scores(acc_banks[p % 2], proj[:, T_QI + p, :], ki_dup).then_inc(idx_dots, 1)
            pe.wait_ge(idx_relu, TILES)
            pe.wait_ge(lat_lo_ready, 3)
            sets = [set_free(), set_free()]
            for r in range(2):
                hi, lo = w_slot(1, SLAB)
                for i in range(TILES):
                    o = acc[sets[i // 4]][:, i % 4, :]
                    c = slice(i * P, (i + 1) * P)
                    mm(o, hi[:, 0, c], lat_hi[:, r, :], start=r == 0 and i % 2 == 0)
                    mm(o, hi[:, 0, c], lat_lo[:, r, :])
                    last = mm(o, lo[:, 0, c], lat_hi[:, r, :], stop=r == 1 and i % 2 == 1)
                last.then_inc(slab_used, 1)
                slabs.step()
            sets = [set_free(), set_free()]
            for r in range(2):
                hi, lo = w_slot(1, SLAB)
                for half in range(HALVES):
                    tok = slice(half * P, (half + 1) * P)
                    for b in range(2):
                        o = acc_banks[sets[half]][:, b, :]
                        c = slice(b * 512, (b + 1) * 512)
                        mm(o, lat_hi[:, r, tok], hi[:, 0, c], start=r == 0)
                        mm(o, lat_hi[:, r, tok], lo[:, 0, c])
                        last = mm(o, lat_lo[:, r, tok], hi[:, 0, c], stop=r == 1)
                last.then_inc(slab_used, 1)
                slabs.step()
            pe.wait_ge(att[0]["mix_lo"], TILES)
            with loop(pe, 2, [(slabs, 8), (macros, 2)]) as i:
                for m in range(2):
                    gemm(4, h_hi, h_lo, four)
            for s in range(2):
                pe.wait_ge(acc_taken[s], (macros.total() + 1 - s) // 2 + 1)
            attention(1)
            pe.wait_ge(att[1]["mix_lo"], TILES)
            with loop(pe, 2, [(slabs, 8), (macros, 2)]) as i:
                for m in range(2):
                    gemm(4, h_hi, h_lo, four, x0=TILES)

            norm_sums()
            ffs = Count()

            def ff_up(before=None):
                for m in range(2):
                    gemm(8, h_hi, h_lo, four, before=before)

            def ff_down(a):
                ffs.step()
                pe.wait_ge(f_lo_ready, ffs.value())
                for m in range(4):
                    gemm(2, f_hi[a], f_lo[a], four)

            ff_up(h_ready(32))
            with loop(pe, FBLOCKS // 2, [(slabs, 48), (macros, 12), (ffs, 2)]) as i:
                for a in range(2):
                    ff_up()
                    ff_down(a)
            ff_down(0)

            norm_sums()
            for s in range(2):
                pe.wait_ge(acc_taken[s], (macros.total() + 1 - s) // 2 + 1)
            for m in range(4):
                pe.wait_ge(fin_ready, m + 1)
                if m >= 2:
                    pe.wait_ge(y_copied, m - 1)
                for half in range(HALVES):
                    for n in range(4):
                        last = pe.transpose(acc_banks[m % 2][:, half, n * P:(n + 1) * P], tmp[m % 2][:, n, half * P:(half + 1) * P], ident)
                last.then_inc(fin_turned, 1)


INPUTS = ("x", "positions", "a_norm_g", "a_w_in", "a_w_group", "a_scale", "a_w_out", "kv_norm_g", "kv_w_a", "kv_latent_g",
          "kv_w_b", "k_norm_g", "b_norm_g", "b_w_in", "b_q_latent_g", "b_w_q_b", "b_q_norm_g", "b_w_out", "c_2",
          "w_mod_2", "b_mod_2", "norm_attn_2", "w_in_2", "attn_sinks_2", "kv_norm_2", "w_uk_2", "w_uv_2", "rel_bias_2",
          "w_out_2", "norm_ffn_2", "w_up_2", "conv_w_2", "conv_b_2", "w_down_2", "norm_final_2")


def kernel(**inputs):
    import concourse.bacc as bacc
    from concourse.bass_utils import run_bass_kernel_spmd

    nc = bacc.Bacc("TRN2", target_bir_lowering=False, num_devices=1)
    consts, cols = constants()
    arrays = {name: np.ascontiguousarray(inputs[name]) for name in INPUTS}
    arrays["consts"] = consts
    dram = {name: nc.dram_tensor(f"in_{name}", a.shape, mybir.dt.from_np(a.dtype), kind="ExternalInput").ap()
            for name, a in arrays.items()}
    out = nc.dram_tensor("out_0", (1, TOK, D), F32, kind="ExternalOutput").ap()
    two_block_kernel(nc, dram, out, cols)
    ran = run_bass_kernel_spmd(nc, [{f"in_{name}": a for name, a in arrays.items()}], core_ids=[0])
    return ran.results[0]["out_0"]
```
